# Optimizing a Trainium2 kernel written in Bass

```python
import math
import jax, jax.numpy as jnp
from jax import lax
import numpy as np

D_MODEL = 1024
BATCH = 1
SEQ = 1024
DEPTH = 2
DEC_BATCH = 8
DEC_SEQ = 4
PAST_LEN = 256
PAGE_SIZE = 128

NSA_HEADS = 8
NSA_KV_HEADS = 2
HEAD_DIM = 64
NSA_WIDTH = NSA_HEADS * HEAD_DIM
NSA_HG = NSA_HEADS // NSA_KV_HEADS
CMP_BLOCK = 32
CMP_HIDDEN = 2 * HEAD_DIM
SEL_BLOCK = 64
TOP_N = 16
WINDOW = 512
Q_BLOCK = 128
FORCE_BONUS = 1.0e4
ROPE_THETA = 10000.0
SSD_HEADS = 16
SSD_HEAD_DIM = 64
SSD_INNER = SSD_HEADS * SSD_HEAD_DIM
SSD_GROUPS = 2
SSD_STATE = 128
SSD_CONV = 4
SSD_CONV_CH = SSD_INNER + 2 * SSD_GROUPS * SSD_STATE
SSD_CHUNK = 64
GLA_HEADS = 4
GLA_DK = 128
GLA_DV = 256
GLA_KEY_WIDTH = GLA_HEADS * GLA_DK
GLA_VAL_WIDTH = GLA_HEADS * GLA_DV
GLA_GATE_RANK = 16
GLA_TAU = 16.0
GLA_CHUNK = 32
N_EVEN = (DEPTH + 1) // 2
N_ODD = DEPTH // 2
EVEN_SPLIT = [NSA_WIDTH, 3 * NSA_HEADS, 6 * NSA_KV_HEADS * HEAD_DIM, NSA_WIDTH,
              SSD_INNER, SSD_CONV_CH, SSD_HEADS]
EVEN_IN = sum(EVEN_SPLIT)
MIX_EVEN = NSA_WIDTH + SSD_INNER
ODD_SPLIT = [GLA_KEY_WIDTH, GLA_KEY_WIDTH, GLA_VAL_WIDTH, GLA_GATE_RANK, GLA_VAL_WIDTH]
ODD_IN = sum(ODD_SPLIT)
F32 = jnp.float32

kernel_name = "nsa_ssd_gla_hybrid_step"

def _split(x, sizes):
    idx = [int(v) for v in np.cumsum(sizes)[:-1]]
    return jnp.split(x, idx, axis=-1)

def rms_norm(x, w, eps=1e-6):
    x32 = x.astype(F32)
    y = x32 * lax.rsqrt(jnp.mean(x32 * x32, axis=-1, keepdims=True) + eps)
    return (y * w.astype(F32)).astype(x.dtype)

def rope(x, pos):
    half = HEAD_DIM // 2
    inv = ROPE_THETA ** (-jnp.arange(half, dtype=F32) / half)
    ang = pos.astype(F32)[:, None] * inv[None, :]
    cos = jnp.cos(ang)[None, :, None, :]
    sin = jnp.sin(ang)[None, :, None, :]
    x32 = x.astype(F32)
    x1, x2 = x32[..., :half], x32[..., half:]
    return jnp.concatenate([x1 * cos - x2 * sin, x1 * sin + x2 * cos], axis=-1).astype(x.dtype)

def masked_softmax(s, mask):
    s = jnp.where(mask, s.astype(F32), -jnp.inf)
    m = jnp.max(s, axis=-1, keepdims=True)
    m = jnp.where(jnp.isfinite(m), m, 0.0)
    p = jnp.exp(s - m)
    d = jnp.sum(p, axis=-1, keepdims=True)
    return p / jnp.where(d > 0, d, 1.0)

def nsa_compress(raw, pe, w1, w2):
    b, l, g, dh = raw.shape
    n = l // CMP_BLOCK
    blk = raw[:, :n * CMP_BLOCK].reshape(b, n, CMP_BLOCK, g, dh) + pe[None, None, :, None, :].astype(raw.dtype)
    flat = blk.transpose(0, 1, 3, 2, 4).reshape(b, n, g, CMP_BLOCK * dh)
    return jax.nn.silu(flat @ w1) @ w2

_gather_blocks = jax.vmap(jax.vmap(lambda kb, ix: kb[ix]))

def nsa_attend_block(q, gates, qpos, kc, vc, ks_blk, vs_blk, kw, vw, wpos):
    b, qb = q.shape[:2]
    scale = HEAD_DIM ** -0.5
    qg = q.reshape(b, qb, NSA_KV_HEADS, NSA_HG, HEAD_DIM)
    nc = kc.shape[1]
    cmp_end = (jnp.arange(nc) + 1) * CMP_BLOCK - 1
    mask_c = cmp_end[None, :] <= qpos[:, None]
    p_c = masked_softmax(jnp.einsum('bqghd,bngd->bghqn', qg, kc) * scale, mask_c)
    o_c = jnp.einsum('bghqn,bngd->bqghd', p_c.astype(vc.dtype), vc)
    ns = ks_blk.shape[2]
    imp = jnp.sum(p_c, axis=2)
    imp = jnp.pad(imp, ((0, 0), (0, 0), (0, 0), (0, 2 * ns - nc)))
    imp = imp.reshape(b, NSA_KV_HEADS, qb, ns, 2).sum(-1)
    blk = jnp.arange(ns)
    cur = qpos // SEL_BLOCK
    forced = (blk[None, :] == 0) | (blk[None, :] == cur[:, None]) | (blk[None, :] == cur[:, None] - 1)
    causal_blk = (blk * SEL_BLOCK)[None, :] <= qpos[:, None]
    imp = jnp.where(forced, imp + FORCE_BONUS, imp)
    imp = jnp.where(causal_blk, imp, -jnp.inf)
    n_top = min(TOP_N, ns)
    _, idx = lax.top_k(imp, n_top)
    kg = _gather_blocks(ks_blk, idx).reshape(b, NSA_KV_HEADS, qb, n_top * SEL_BLOCK, HEAD_DIM)
    vg = _gather_blocks(vs_blk, idx).reshape(b, NSA_KV_HEADS, qb, n_top * SEL_BLOCK, HEAD_DIM)
    key_pos = (idx[..., None] * SEL_BLOCK + jnp.arange(SEL_BLOCK)).reshape(b, NSA_KV_HEADS, qb, n_top * SEL_BLOCK)
    mask_s = (key_pos <= qpos[None, None, :, None])[:, :, None]
    p_s = masked_softmax(jnp.einsum('bqghd,bgqkd->bghqk', qg, kg) * scale, mask_s)
    o_s = jnp.einsum('bghqk,bgqkd->bqghd', p_s.astype(vg.dtype), vg)
    dist = qpos[:, None] - wpos[None, :]
    mask_w = (dist >= 0) & (dist < WINDOW) & (wpos >= 0)[None, :]
    p_w = masked_softmax(jnp.einsum('bqghd,blgd->bghql', qg, kw) * scale, mask_w)
    o_w = jnp.einsum('bghql,blgd->bqghd', p_w.astype(vw.dtype), vw)
    g = gates.reshape(b, qb, 3, NSA_KV_HEADS, NSA_HG, 1)
    o = g[:, :, 0] * o_c + g[:, :, 1] * o_s + g[:, :, 2] * o_w
    return o.reshape(b, qb, NSA_WIDTH).astype(q.dtype)

def nsa_mixer(q_raw, g_raw, kv_raw, pos, pe, w1, w2, past_kv, past_win):
    b, s, _ = q_raw.shape
    q = rope(q_raw.reshape(b, s, NSA_HEADS, HEAD_DIM), pos)
    gates = jax.nn.sigmoid(g_raw.astype(F32)).reshape(b, s, 3, NSA_HEADS)
    kv = kv_raw.reshape(b, s, 6, NSA_KV_HEADS, HEAD_DIM)
    k_cmp = rope(kv[:, :, 0], pos)
    k_slc = rope(kv[:, :, 2], pos)
    k_win = rope(kv[:, :, 4], pos)
    new_kv = jnp.stack([k_cmp, kv[:, :, 1], k_slc, kv[:, :, 3]], axis=2)
    new_win = jnp.stack([k_win, kv[:, :, 5]], axis=2)
    if past_kv is None:
        full_kv, win_kv = new_kv, new_win
        win_keep = min(WINDOW, s)
    else:
        full_kv = jnp.concatenate([past_kv.astype(new_kv.dtype), new_kv], axis=1)
        win_kv = jnp.concatenate([past_win.astype(new_win.dtype), new_win], axis=1)
        win_keep = past_win.shape[1]
    L = full_kv.shape[1]
    kc = nsa_compress(full_kv[:, :, 0], pe[0], w1[0], w2[0])
    vc = nsa_compress(full_kv[:, :, 1], pe[1], w1[1], w2[1])
    ns = -(-L // SEL_BLOCK)
    sel = jnp.pad(full_kv[:, :, 2:4], ((0, 0), (0, ns * SEL_BLOCK - L), (0, 0), (0, 0), (0, 0)))
    sel = sel.reshape(b, ns, SEL_BLOCK, 2, NSA_KV_HEADS, HEAD_DIM).transpose(3, 0, 4, 1, 2, 5)
    ks_blk, vs_blk = sel[0], sel[1]
    if past_kv is None:
        nb = s // Q_BLOCK
        win_pad = jnp.pad(win_kv, ((0, 0), (WINDOW, 0), (0, 0), (0, 0), (0, 0)))

        def one_block(args):
            qb_, gb_, q0 = args
            qpos = q0 + jnp.arange(Q_BLOCK, dtype=jnp.int32)
            wkv = lax.dynamic_slice_in_dim(win_pad, q0, WINDOW + Q_BLOCK, axis=1)
            wpos = q0 - WINDOW + jnp.arange(WINDOW + Q_BLOCK, dtype=jnp.int32)
            return nsa_attend_block(qb_, gb_, qpos, kc, vc, ks_blk, vs_blk, wkv[:, :, 0], wkv[:, :, 1], wpos)

        qs = q.reshape(b, nb, Q_BLOCK, NSA_HEADS, HEAD_DIM).swapaxes(0, 1)
        gs = gates.reshape(b, nb, Q_BLOCK, 3, NSA_HEADS).swapaxes(0, 1)
        out = lax.map(one_block, (qs, gs, jnp.arange(nb, dtype=jnp.int32) * Q_BLOCK))
        out = out.swapaxes(0, 1).reshape(b, s, NSA_WIDTH)
    else:
        past_len = past_kv.shape[1]
        wpos = past_len - win_keep + jnp.arange(win_keep + s, dtype=jnp.int32)
        out = nsa_attend_block(q, gates, pos, kc, vc, ks_blk, vs_blk, win_kv[:, :, 0], win_kv[:, :, 1], wpos)
    return out, new_kv, win_kv[:, -win_keep:]

def _chunked(t, n, c, pad):
    t = jnp.pad(t.astype(F32), [(0, 0), (0, pad)] + [(0, 0)] * (t.ndim - 2))
    return t.reshape((t.shape[0], n, c) + t.shape[2:]).swapaxes(0, 1)

def ssd_scan(x, dt, a, bm, cm, h0):
    b, s = x.shape[:2]
    c = min(SSD_CHUNK, s)
    n = -(-s // c)
    pad = n * c - s
    hg = SSD_HEADS // SSD_GROUPS
    xs = (_chunked(x, n, c, pad), _chunked(dt, n, c, pad), _chunked(bm, n, c, pad), _chunked(cm, n, c, pad))
    tri = jnp.tril(jnp.ones((c, c), bool))[None, :, :, None]

    def step(h, inp):
        xc, dtc, bc, cc = inp
        cum = jnp.cumsum(dtc * a, axis=1)
        xdt = xc * dtc[..., None]
        diff = cum[:, :, None, :] - cum[:, None, :, :]
        lmat = jnp.where(tri, jnp.exp(jnp.where(tri, diff, 0.0)), 0.0)
        cb = jnp.repeat(jnp.einsum('btgn,bsgn->btsg', cc, bc), hg, axis=-1)
        ch = jnp.repeat(cc, hg, axis=2)
        bh = jnp.repeat(bc, hg, axis=2)
        y = jnp.einsum('btsh,bshp->bthp', cb * lmat, xdt) \
            + jnp.einsum('bthn,bhpn->bthp', ch, h) * jnp.exp(cum)[..., None]
        decay_out = jnp.exp(cum[:, -1:, :] - cum)
        h = h * jnp.exp(cum[:, -1])[:, :, None, None] \
            + jnp.einsum('bshn,bshp->bhpn', bh * decay_out[..., None], xdt)
        return h, y

    h, ys = lax.scan(step, h0.astype(F32), xs)
    y = ys.swapaxes(0, 1).reshape(b, n * c, SSD_HEADS, SSD_HEAD_DIM)[:, :s]
    return y, h

def gla_scan(q, k, v, lg, s0):
    b, s = q.shape[:2]
    c = min(GLA_CHUNK, s)
    n = -(-s // c)
    pad = n * c - s
    xs = (_chunked(q, n, c, pad), _chunked(k, n, c, pad), _chunked(v, n, c, pad), _chunked(lg, n, c, pad))
    tri = jnp.tril(jnp.ones((c, c), bool))[None, None]

    def step(st, inp):
        qc, kc, vc, gc = inp
        bcum = jnp.cumsum(gc, axis=1)
        qg = qc * jnp.exp(bcum)
        kg = kc * jnp.exp(-bcum)
        att = jnp.where(tri, jnp.einsum('bthd,bshd->bhts', qg, kg), 0.0)
        o = jnp.einsum('bhts,bshv->bthv', att, vc) + jnp.einsum('bthd,bhdv->bthv', qg, st)
        blast = bcum[:, -1]
        st = st * jnp.exp(blast)[..., None] \
            + jnp.einsum('bshd,bshv->bhdv', kc * jnp.exp(blast[:, None] - bcum), vc)
        return st, o

    st, os_ = lax.scan(step, s0.astype(F32), xs)
    o = os_.swapaxes(0, 1).reshape(b, n * c, GLA_HEADS, GLA_DV)[:, :s]
    return o, st

def even_layer(h, pos, e, W, past):
    b, s, _ = h.shape
    proj = h @ W["w_in_even"][e]
    q_a, g_a, kv_a, z_a, z_b, xbc, dt_raw = _split(proj, EVEN_SPLIT)
    if past is None:
        past_kv = past_win = None
        prev = jnp.zeros((b, SSD_CONV - 1, SSD_CONV_CH), h.dtype)
        h0 = jnp.zeros((b, SSD_HEADS, SSD_HEAD_DIM, SSD_STATE), F32)
    else:
        past_kv, past_win, prev, h0 = past
    o_a, new_kv, new_win = nsa_mixer(q_a, g_a, kv_a, pos, W["nsa_cmp_pe"][e], W["nsa_cmp_w1"][e],
                                     W["nsa_cmp_w2"][e], past_kv, past_win)
    o_a = o_a * jax.nn.silu(z_a)
    xp = jnp.concatenate([prev.astype(xbc.dtype), xbc], axis=1)
    cw = W["ssd_conv_w"][e]
    conv = W["ssd_conv_b"][e]
    for i in range(SSD_CONV):
        conv = conv + xp[:, i:i + s] * cw[i]
    new_conv = xp[:, -(SSD_CONV - 1):]
    xs, bm, cm = _split(jax.nn.silu(conv), [SSD_INNER, SSD_GROUPS * SSD_STATE, SSD_GROUPS * SSD_STATE])
    xs = xs.reshape(b, s, SSD_HEADS, SSD_HEAD_DIM)
    dt = jax.nn.softplus(dt_raw.astype(F32) + W["ssd_dt_bias"][e].astype(F32))
    a = -jnp.exp(W["ssd_a_log"][e].astype(F32))
    y, new_ssd = ssd_scan(xs, dt, a, bm.reshape(b, s, SSD_GROUPS, SSD_STATE),
                          cm.reshape(b, s, SSD_GROUPS, SSD_STATE), h0)
    y = y + xs.astype(F32) * W["ssd_d"][e].astype(F32)[:, None]
    y = y.reshape(b, s, SSD_INNER) * jax.nn.silu(z_b.astype(F32))
    y = rms_norm(y, W["ssd_norm_w"][e]).astype(h.dtype)
    out = jnp.concatenate([o_a.astype(h.dtype), y], axis=-1) @ W["w_out_even"][e]
    return out, (new_kv, new_win, new_conv, new_ssd.astype(h.dtype))

def odd_layer(h, o_idx, W, past):
    b, s, _ = h.shape
    proj = h @ W["w_in_odd"][o_idx]
    q, k, v, glr, r = _split(proj, ODD_SPLIT)
    q = q.reshape(b, s, GLA_HEADS, GLA_DK) * (GLA_DK ** -0.5)
    k = k.reshape(b, s, GLA_HEADS, GLA_DK)
    v = v.reshape(b, s, GLA_HEADS, GLA_DV)
    lg = jax.nn.log_sigmoid((glr @ W["gla_w_gate2"][o_idx] + W["gla_b_gate"][o_idx]).astype(F32)) / GLA_TAU
    lg = lg.reshape(b, s, GLA_HEADS, GLA_DK)
    s0 = jnp.zeros((b, GLA_HEADS, GLA_DK, GLA_DV), F32) if past is None else past
    o, st = gla_scan(q, k, v, lg, s0)
    o = rms_norm(o, W["gla_norm_w"][o_idx]).reshape(b, s, GLA_VAL_WIDTH)
    o = (o * jax.nn.silu(r.astype(F32))).astype(h.dtype)
    return o @ W["w_out_odd"][o_idx], st.astype(h.dtype)

def apply_layer(x, c, pos, l, W, past):
    mod = jax.nn.silu(c) @ W["w_mod"][l] + W["b_mod"][l]
    shift, scale, gate = jnp.split(mod[:, None, :], 3, axis=-1)
    h = rms_norm(x, W["norm_w"][l]) * (1 + scale) + shift
    if l % 2 == 0:
        out, st = even_layer(h, pos, l // 2, W, past)
    else:
        out, st = odd_layer(h, l // 2, W, past)
    return x + gate * out, st

def setup_inputs(seed: int = 0) -> dict:
    key = jax.random.key(seed)
    kit = iter(list(jax.random.split(key, 40)))

    def nrm(shape, scale):
        return jax.random.normal(next(kit), shape, F32) * scale

    n_pages = PAST_LEN // PAGE_SIZE
    n_used = DEC_BATCH * n_pages
    n_pool = n_used + -(-n_used // 4)
    win_keep = min(WINDOW, PAST_LEN)
    d = D_MODEL
    inp = {}
    inp["x_prompt"] = nrm((BATCH, SEQ, d), 1.0)
    inp["x_sample"] = nrm((DEC_BATCH, DEC_SEQ, d), 1.0)
    inp["c_prompt"] = nrm((BATCH, d), 1.0)
    inp["c_sample"] = nrm((DEC_BATCH, d), 1.0)
    inp["cache_nsa"] = nrm((N_EVEN, n_pool, PAGE_SIZE, 4, NSA_KV_HEADS, HEAD_DIM), 1.0)
    inp["cache_nsa_win"] = nrm((N_EVEN, DEC_BATCH, win_keep, 2, NSA_KV_HEADS, HEAD_DIM), 1.0)
    inp["state_ssd_conv"] = nrm((N_EVEN, DEC_BATCH, SSD_CONV - 1, SSD_CONV_CH), 1.0)
    inp["state_ssd"] = nrm((N_EVEN, DEC_BATCH, SSD_HEADS, SSD_HEAD_DIM, SSD_STATE), 0.1)
    inp["state_gla"] = nrm((N_ODD, DEC_BATCH, GLA_HEADS, GLA_DK, GLA_DV), 0.1)
    inp["page_table"] = jax.random.permutation(next(kit), n_pool)[:n_used].reshape(DEC_BATCH, n_pages).astype(jnp.int32)
    inp["norm_w"] = 1.0 + nrm((DEPTH, d), 0.02)
    inp["w_mod"] = nrm((DEPTH, d, 3 * d), 0.5 * d ** -0.5)
    inp["b_mod"] = nrm((DEPTH, 3 * d), 0.02)
    inp["w_in_even"] = nrm((N_EVEN, d, EVEN_IN), d ** -0.5)
    inp["w_out_even"] = nrm((N_EVEN, MIX_EVEN, d), MIX_EVEN ** -0.5)
    inp["nsa_cmp_pe"] = nrm((N_EVEN, 2, CMP_BLOCK, HEAD_DIM), 0.1)
    inp["nsa_cmp_w1"] = nrm((N_EVEN, 2, CMP_BLOCK * HEAD_DIM, CMP_HIDDEN), (CMP_BLOCK * HEAD_DIM) ** -0.5)
    inp["nsa_cmp_w2"] = nrm((N_EVEN, 2, CMP_HIDDEN, HEAD_DIM), CMP_HIDDEN ** -0.5)
    inp["ssd_conv_w"] = nrm((N_EVEN, SSD_CONV, SSD_CONV_CH), SSD_CONV ** -0.5)
    inp["ssd_conv_b"] = nrm((N_EVEN, SSD_CONV_CH), 0.02)
    dt0 = jnp.exp(jax.random.uniform(next(kit), (N_EVEN, SSD_HEADS), F32,
                                     minval=math.log(1e-3), maxval=math.log(1e-1)))
    inp["ssd_dt_bias"] = dt0 + jnp.log(-jnp.expm1(-dt0))
    inp["ssd_a_log"] = jnp.log(jax.random.uniform(next(kit), (N_EVEN, SSD_HEADS), F32, minval=1.0, maxval=16.0))
    inp["ssd_d"] = 1.0 + nrm((N_EVEN, SSD_HEADS), 0.02)
    inp["ssd_norm_w"] = 1.0 + nrm((N_EVEN, SSD_INNER), 0.02)
    inp["w_in_odd"] = nrm((N_ODD, d, ODD_IN), d ** -0.5)
    inp["gla_w_gate2"] = nrm((N_ODD, GLA_GATE_RANK, GLA_KEY_WIDTH), GLA_GATE_RANK ** -0.5)
    inp["gla_b_gate"] = nrm((N_ODD, GLA_KEY_WIDTH), 0.02)
    inp["gla_norm_w"] = 1.0 + nrm((N_ODD, GLA_DV), 0.02)
    inp["w_out_odd"] = nrm((N_ODD, GLA_VAL_WIDTH, d), GLA_VAL_WIDTH ** -0.5)
    inp["final_norm_w"] = 1.0 + nrm((d,), 0.02)
    return inp

def reference(x_prompt, x_sample, c_prompt, c_sample, cache_nsa, cache_nsa_win, state_ssd_conv, state_ssd,
              state_gla, page_table, norm_w, w_mod, b_mod, w_in_even, w_out_even, nsa_cmp_pe, nsa_cmp_w1,
              nsa_cmp_w2, ssd_conv_w, ssd_conv_b, ssd_dt_bias, ssd_a_log, ssd_d, ssd_norm_w, w_in_odd,
              gla_w_gate2, gla_b_gate, gla_norm_w, w_out_odd, final_norm_w):
    W = dict(norm_w=norm_w, w_mod=w_mod, b_mod=b_mod, w_in_even=w_in_even, w_out_even=w_out_even,
             nsa_cmp_pe=nsa_cmp_pe, nsa_cmp_w1=nsa_cmp_w1, nsa_cmp_w2=nsa_cmp_w2, ssd_conv_w=ssd_conv_w,
             ssd_conv_b=ssd_conv_b, ssd_dt_bias=ssd_dt_bias, ssd_a_log=ssd_a_log, ssd_d=ssd_d,
             ssd_norm_w=ssd_norm_w, w_in_odd=w_in_odd, gla_w_gate2=gla_w_gate2, gla_b_gate=gla_b_gate,
             gla_norm_w=gla_norm_w, w_out_odd=w_out_odd)
    dec_b = x_sample.shape[0]
    past_len = page_table.shape[1] * PAGE_SIZE
    pos_p = jnp.arange(x_prompt.shape[1], dtype=jnp.int32)
    pos_s = past_len + jnp.arange(x_sample.shape[1], dtype=jnp.int32)
    hp, hs = x_prompt, x_sample
    kv_p, kv_s, win_p, win_s, cv_p, cv_s, ss_p, ss_s, gl_p, gl_s = ([] for _ in range(10))
    for l in range(DEPTH):
        e = l // 2
        if l % 2 == 0:
            past_kv = cache_nsa[e][page_table].reshape(dec_b, past_len, 4, NSA_KV_HEADS, HEAD_DIM)
            past = (past_kv, cache_nsa_win[e], state_ssd_conv[e], state_ssd[e])
            hp, st_p = apply_layer(hp, c_prompt, pos_p, l, W, None)
            hs, st_s = apply_layer(hs, c_sample, pos_s, l, W, past)
            kv_p.append(st_p[0]); win_p.append(st_p[1]); cv_p.append(st_p[2]); ss_p.append(st_p[3])
            kv_s.append(st_s[0]); win_s.append(st_s[1]); cv_s.append(st_s[2]); ss_s.append(st_s[3])
        else:
            hp, st_p = apply_layer(hp, c_prompt, pos_p, l, W, None)
            hs, st_s = apply_layer(hs, c_sample, pos_s, l, W, state_gla[e])
            gl_p.append(st_p); gl_s.append(st_s)
    y_prompt = rms_norm(hp, final_norm_w)
    y_sample = rms_norm(hs, final_norm_w)
    nsa_rows_prompt = jnp.stack(kv_p)
    nsa_rows_sample = jnp.stack(kv_s)
    nsa_win_prompt = jnp.stack(win_p)
    nsa_win_sample = jnp.stack(win_s)
    ssd_conv_prompt = jnp.stack(cv_p)
    ssd_conv_sample = jnp.stack(cv_s)
    ssd_state_prompt = jnp.stack(ss_p)
    ssd_state_sample = jnp.stack(ss_s)
    gla_state_prompt = jnp.stack(gl_p)
    gla_state_sample = jnp.stack(gl_s)
    return (y_prompt, y_sample, nsa_rows_prompt, nsa_rows_sample, nsa_win_prompt, nsa_win_sample,
            ssd_conv_prompt, ssd_conv_sample, ssd_state_prompt, ssd_state_sample,
            gla_state_prompt, gla_state_sample)


_drawn_inputs = setup_inputs


def setup_inputs(seed=0):
    import zlib

    import numpy as np

    out = dict(_drawn_inputs(seed))
    spreads = {}
    factors = {'nsa_cmp_pe': 8.0,
     'nsa_cmp_w1': 3.007,
     'ssd_d': 8.0,
     'ssd_norm_w': 8.0,
     'gla_b_gate': 6.352,
     'gla_norm_w': 8.0,
     'final_norm_w': 2.929}
    for name, (base, spread) in spreads.items():
        noise = np.random.default_rng([zlib.crc32(name.encode()), seed]).standard_normal(out[name].shape)
        drawn = base * np.exp(spread * noise) if base else spread * noise
        out[name] = __import__('jax').numpy.asarray(drawn.astype(out[name].dtype))
    for name, factor in factors.items():
        out[name] = (out[name] * factor).astype(out[name].dtype)
    return out
```

```python
from contextlib import ExitStack

import numpy as np

import concourse.bass as bass
from concourse import mybir

F32 = mybir.dt.float32
F32R = mybir.dt.float32r
BF16 = mybir.dt.bfloat16
I32 = mybir.dt.int32
ALU = mybir.AluOpType
ACT = mybir.ActivationFunctionType
AX = mybir.AxisListType

P = 128
D = 1024
KD = D // P
TP = 1024
DB, DS = 8, 4
TS = DB * DS
T = TP + TS
NTP = TP // P
NT = NTP + 1
PAST = 256
PAGE = 128
NPG = PAST // PAGE
NPOOL = 20
H, G, HD = 8, 2, 64
HG = H // G
CB = 32
NCP = TP // CB
NCS = PAST // CB
WIN = 512
SH, SP_, SN = 16, 64, 128
SI = SH * SP_
CCH = SI + 2 * 2 * SN
KC = CCH // P
LH, LK, LV = 4, 128, 256
LC = 32
EPS = 1e-6
NEG = -1e30
SCALE = HD ** -0.5
E_Q, E_G, E_KV, E_ZA, E_ZB, E_XBC, E_DT, E_END = 0, 512, 536, 1304, 1816, 2840, 4376, 4392
O_Q, O_K, O_V, O_GLR, O_R, O_END = 0, 512, 1024, 2048, 2064, 3088
CHUNKS = [(c * T // 3, T // 3) for c in range(3)]
LAST = TP - CHUNKS[2][0]
ATTN_COLS = [(E_Q, 512), (E_G, 408), (E_G + 408, 384)]
KT_PROMPT, KT_PAST = 0, TP
NKEY = TP + DB * PAST


def rows(m):
    return P if m < NTP else TS


F_COLS = {}
_at = 0
for _n, _w in (("ident", 128), ("tri", 128), ("tri32", 128), ("trib", 32), ("oneb", 32), ("bcol", 8),
               ("bmask", 256), ("valid", 1), ("own", 2)):
    F_COLS[_n] = (_at, _at + _w)
    _at += _w
F_WIDTH = _at
B_COLS = {"ident": (0, 128), "causal": (128, 256), "old": (256, 384), "cmp": (384, 384 + 8 * NCP),
          "new": (384 + 8 * NCP, 384 + 8 * NCP + 64), "later": (704, 832), "laterb": (832, 864)}
B_WIDTH = 864


def shape_constants():
    f = np.zeros((P, F_WIDTH), np.float32)
    p = np.arange(P)

    def put(a, cols, name, v):
        s, e = cols[name]
        v = np.asarray(v, np.float32)
        a[: v.shape[0], s:e] = v.reshape(v.shape[0], e - s)

    t32 = np.arange(TS)
    put(f, F_COLS, "ident", np.eye(P))
    put(f, F_COLS, "tri", p[:, None] <= p[None, :])
    put(f, F_COLS, "tri32", (p[:, None] <= p[None, :]) & (p[:, None] // LC == p[None, :] // LC))
    same = t32[:, None] // DS == t32[None, :] // DS
    put(f, F_COLS, "trib", same & (t32[:, None] <= t32[None, :]))
    put(f, F_COLS, "oneb", same)
    put(f, F_COLS, "bcol", t32[:, None] // DS == np.arange(DB)[None, :])
    bm = (t32[None, :] // DS == np.arange(DB)[:, None]).reshape(1, DB * TS)
    put(f, F_COLS, "bmask", np.broadcast_to(bm, (P, DB * TS)))
    put(f, F_COLS, "valid", (p >= CB - 1)[:, None])
    g = (p // (HG * DS)) % G
    put(f, F_COLS, "own", g[:, None] == np.arange(G)[None, :])
    b = np.zeros((P, B_WIDTH), np.float32)
    put(b, B_COLS, "ident", np.eye(P))
    put(b, B_COLS, "causal", np.where(p[None, :] <= p[:, None], 0, NEG))
    put(b, B_COLS, "old", np.where(p[None, :] > p[:, None], 0, NEG))
    q = np.arange(NTP)[None, :, None] * P + p[:, None, None]
    ce = (np.arange(NCP) + 1) * CB - 1
    put(b, B_COLS, "cmp", np.where(ce[None, None, :] <= q, 0, NEG).reshape(P, NTP * NCP))
    rb, rt = p // (H * DS), p % DS
    new = [np.where((t32[None, :] // DS == 4 * f2 + rb[:, None]) & (t32[None, :] % DS <= rt[:, None]), 0, NEG)
           for f2 in range(2)]
    put(b, B_COLS, "new", np.stack(new, 1).reshape(P, 2 * TS))
    put(b, B_COLS, "later", np.where(p[:, None] <= p[None, :], 0, NEG))
    put(b, B_COLS, "laterb", np.where(same & (t32[:, None] <= t32[None, :]), 0, NEG))
    half = HD // 2
    inv = np.float32(10000.0) ** (-np.arange(half, dtype=np.float32) / np.float32(half))
    pos = np.zeros((P, NT), np.float32)
    pos[:, :NTP] = np.arange(NTP)[None, :] * P + p[:, None]
    pos[:TS, NTP] = PAST + t32 % DS
    ang = pos[:, :, None] * inv.astype(np.float32)[None, None, :]
    cos, sin = np.cos(ang), np.sin(ang)
    rope = np.stack([np.concatenate([cos, cos], -1), np.concatenate([-sin, sin], -1)], 1).astype(np.float32)
    scan = np.ones((P, T), np.float32)
    scan[:, 0:TP:LC] = 0
    scan[:, TP::DS] = 0
    return {"k_f32": f, "k_masks": b, "k_rope": rope.reshape(P, -1), "k_scan": scan}
BLOCK_SEMS = []


def new_sem(nc, name):
    BLOCK_SEMS.append(nc.alloc_semaphore(name))
    return BLOCK_SEMS[-1]


def end_block(nc):
    nc.clear_and_free_semaphores(list(BLOCK_SEMS))
    nc.all_engine_barrier()
    BLOCK_SEMS.clear()


class Env:
    pass


def bank(e, b, n=512):
    return e.ps[:, b, 0:n]


def mm(nc, out, lhsT, rhs, start, stop):
    return nc.tensor.matmul(out, lhsT, rhs, start=start, stop=stop, skip_group_check=True)


def make_link(eng, sem, count):
    def link(ins):
        count[0] += 1
        ins.then_inc(sem, 1)
        eng.wait_ge(sem, count[0])
    return link


VEC = {}
_at = 0
for _n, _w in (("b_mod", 48), ("norm_w", 16), ("final_w", 8), ("ssd_norm", 8), ("gla_norm", 2), ("gla_b", 4),
               ("conv_b", KC)):
    VEC[_n] = (_at, _at + _w)
    _at += _w
NVEC = _at
NCW = 4 * KC


def load_mod_half(eng, e, l, kind, half, buf, sem):
    s = kind * D + half * 512
    eng.dma_start(buf, e.w_mod[l, :, s:s + 512].rearrange("(k p) n -> p k n", p=P)).then_inc(sem, 16)


def mod_products(nc, e, buf, b):
    for k in range(KD):
        last = mm(nc, e.ps[0:9, b, :], e.cT[:, k, :], buf[:, k, :], k == 0, k == KD - 1)
    return last


def mod_turn(nc, e, mrow, b, at):
    for f in range(KD):
        last = nc.tensor.transpose(e.ps[:, b, at + 9 * f:at + 9 * (f + 1)], mrow[:, f * P:(f + 1) * P], e.ident[0:9, 0:9])
    return last


def mod_finish(nc, e, link, l, kind, b, at):
    s = VEC["b_mod"][0] + 24 * l + 8 * kind
    out = e.mod[:, l, 8 * kind:8 * kind + 8, :]
    link(nc.vector.tensor_tensor(out, e.ps[:, b, at:at + 72].rearrange("p (f c) -> p f c", c=9), e.vec[:, s:s + 8][:, :, None].broadcast_to([P, 8, 9]), ALU.add))
    if kind == 1:
        s = VEC["norm_w"][0] + 8 * l
        link(nc.vector.scalar_tensor_tensor(out, out, 1.0, e.vec[:, s:s + 8][:, :, None].broadcast_to([P, 8, 9]), ALU.add, ALU.mult))


def load_attn_w(eng, e, w, sem, cols):
    s, n = cols
    eng.dma_start(w[:, :, 0:n], e.w_in_even[0].rearrange("(k p) n -> p k n", p=P)[:, :, s:s + n]).then_inc(sem, 16)


def block_load(nc, e, xT, hT):
    with ExitStack() as ctx:
        xin = ctx.enter_context(nc.sbuf_tensor("xin", [P, NT, D], F32))
        wm = [hT[:, :, 0:D], ctx.enter_context(nc.sbuf_tensor("w_mod_rows", [P, KD, D], F32))[:, :, :]]
        cin = ctx.enter_context(nc.sbuf_tensor("c_rows", [9, D], F32))
        cT = e.cT
        vrows = ctx.enter_context(nc.sbuf_tensor("vec_rows", [NVEC, P], F32))
        wrows = ctx.enter_context(nc.sbuf_tensor("conv_w_rows", [NCW, P], F32))
        mrow = ctx.enter_context(nc.sbuf_tensor("mod_rows", [9, D], F32))
        masks = ctx.enter_context(nc.sbuf_tensor("mask_rows", [P, B_WIDTH], F32))
        masks_ready = new_sem(nc, "masks_ready")
        consts_in, c_in, vec_in = new_sem(nc, "consts_in"), new_sem(nc, "c_in"), new_sem(nc, "vec_in")
        x_in = [new_sem(nc, f"x_in{i}") for i in range(3)]
        wmod_in = [new_sem(nc, f"w_mod_in{i}") for i in range(2)]
        xt_done, xt_copied = new_sem(nc, "x_transposed"), new_sem(nc, "x_T_copied")
        cv_done, c_ready = new_sem(nc, "c_vec_transposed"), new_sem(nc, "c_T_ready")
        mod_done, mod_rows, mod_turned = new_sem(nc, "mod_done"), new_sem(nc, "mod_rows_ready"), new_sem(nc, "mod_turned")
        mod_taken = new_sem(nc, "mod_taken")
        xT_saved = new_sem(nc, "x_T_saved")
        NG = NT * 2

        with nc.Block() as block:
            @block.sync
            def _(sp):
                sp.dma_start(e.kf[:, :], e.k_f32).then_inc(consts_in, 16)
                sp.dma_start(masks[:, :], e.k_masks).then_inc(consts_in, 16)
                sp.dma_start(cin[0:1, :], e.c_prompt).then_inc(c_in, 16)
                sp.dma_start(cin[1:9, :], e.c_sample).then_inc(c_in, 16)
                xp = e.x_prompt.rearrange("b (m p) d -> p (b m) d", p=P)
                sp.dma_start(xin[:, 0:4, :], xp[:, 0:4, :]).then_inc(x_in[0], 16)
                sp.dma_start(xin[:, 4:8, :], xp[:, 4:8, :]).then_inc(x_in[1], 16)
                sp.dma_start(xin[0:TS, 8, :], e.x_sample.rearrange("b t d -> (b t) d")).then_inc(x_in[2], 16)
                for i in range(2):
                    for half in range(2):
                        load_mod_half(sp, e, 0, i, half, wm[i][:, :, half * 512:(half + 1) * 512], wmod_in[i])
                for i in range(2):
                    load_attn_w(sp, e, e.w_attn[:, i], e.w_attn_in[i], ATTN_COLS[i])
                sp.wait_ge(xt_copied, NG)
                sp.dma_start(e.x_save, xT[:, :, :]).then_inc(xT_saved, 16)
                sp.wait_ge(xT_saved, 16)

            @block.gpsimd
            def _(pool):
                for name, src in (("b_mod", e.b_mod.rearrange("l (f p) -> (l f) p", p=P)),
                                  ("norm_w", e.norm_w.rearrange("l (f p) -> (l f) p", p=P)),
                                  ("final_w", e.final_norm_w.rearrange("(f p) -> f p", p=P)),
                                  ("ssd_norm", e.ssd_norm_w.rearrange("l (f p) -> (l f) p", p=P)),
                                  ("gla_norm", e.gla_norm_w.rearrange("l (f p) -> (l f) p", p=P)),
                                  ("gla_b", e.gla_b_gate.rearrange("l (f p) -> (l f) p", p=P)),
                                  ("conv_b", e.ssd_conv_b.rearrange("l (f p) -> (l f) p", p=P))):
                    s, t = VEC[name]
                    pool.dma_start(vrows[s:t, :], src).then_inc(vec_in, 16)
                pool.dma_start(wrows[:, :], e.ssd_conv_w.rearrange("l i (f p) -> (l i f) p", p=P)).then_inc(vec_in, 16)
                pool.dma_start(e.ssd_row[:, 0, :], e.ssd_dt_bias.partition_broadcast(P).rearrange("p l h -> p (l h)")).then_inc(vec_in, 16)
                pool.dma_start(e.ssd_row[:, 1, :], e.ssd_a_log.partition_broadcast(P).rearrange("p l h -> p (l h)")).then_inc(vec_in, 16)
                pool.dma_start(e.ssd_row[:, 2, :], e.ssd_d.partition_broadcast(P).rearrange("p l h -> p (l h)")).then_inc(vec_in, 16)

            @block.tensor
            def _(pe):
                pe.wait_ge(consts_in, 32)
                pe.wait_ge(c_in, 32)
                for k in range(KD):
                    last = nc.tensor.transpose(e.ps[:, 4, k * 9:(k + 1) * 9], cin[:, k * P:(k + 1) * P], e.ident[0:9, 0:9])
                last.then_inc(cv_done, 1)
                for g in range(NG):
                    m, half = g // 2, g % 2
                    r = rows(m)
                    if half == 0:
                        pe.wait_ge(x_in[m // 4], 16)
                    if g >= 4:
                        pe.wait_ge(xt_copied, g - 3)
                    for j in range(4):
                        k = 4 * half + j
                        last = nc.tensor.transpose(e.ps[:, g % 4, j * P:j * P + r], xin[0:r, m, k * P:(k + 1) * P], e.ident[0:r, 0:r])
                    last.then_inc(xt_done, 1)
                pe.wait_ge(vec_in, 16 * 11)
                nc.tensor.transpose(e.ps[:, 5, 0:NVEC], vrows[:, :], e.ident[0:NVEC, 0:NVEC])
                nc.tensor.transpose(e.ps[:, 5, NVEC:NVEC + NCW], wrows[:, :], e.ident[0:NCW, 0:NCW]).then_inc(cv_done, 1)
                pe.wait_ge(c_ready, 1)
                for i in range(2):
                    pe.wait_ge(wmod_in[i], 32)
                    if i:
                        pe.wait_ge(mod_rows, i)
                    mod_products(nc, e, wm[i][:, :, 0:512], 6)
                    mod_products(nc, e, wm[i][:, :, 512:1024], 7).then_inc(mod_done, 1)
                    pe.wait_ge(mod_rows, i + 1)
                    if i:
                        pe.wait_ge(mod_taken, i)
                    mod_turn(nc, e, mrow, 4, 0).then_inc(mod_turned, 1)

            @block.scalar
            def _(act):
                act.wait_ge(cv_done, 1)
                nc.scalar.activation(cT[:, :, :], e.ps[:, 4, 0:72].rearrange("p (k c) -> p k c", k=KD), ACT.Silu).then_inc(c_ready, 1)
                for g in range(1, NG, 2):
                    act.wait_ge(xt_done, g + 1)
                    m, r = g // 2, rows(g // 2)
                    act.wait_ge(xt_copied, g)
                    nc.scalar.copy(xT[:, 4:8, m * P:m * P + r], e.ps[:, g % 4, :].rearrange("p (k t) -> p k t", k=4)[:, :, 0:r]).then_inc(xt_copied, 1)

                for i in range(2):
                    act.wait_ge(mod_done, i + 1)
                    if i:
                        act.wait_ge(mod_turned, i)
                    nc.scalar.copy(mrow[:, :].rearrange("p (b n) -> p b n", b=2), e.ps[0:9, 6:8, :]).then_inc(mod_rows, 1)

            @block.vector
            def _(dve):
                link = make_link(dve, e.dve_step, e.dve_n)
                dve.wait_ge(consts_in, 32)
                nc.vector.tensor_copy(e.kb[:, :], masks[:, :]).then_inc(masks_ready, 1)
                for g in range(0, NG, 2):
                    dve.wait_ge(xt_done, g + 1)
                    if g:
                        dve.wait_ge(xt_copied, g)
                    m, r = g // 2, rows(g // 2)
                    nc.vector.tensor_copy(xT[:, 0:4, m * P:m * P + r], e.ps[:, g % 4, :].rearrange("p (k t) -> p k t", k=4)[:, :, 0:r]).then_inc(xt_copied, 1)
                dve.wait_ge(cv_done, 2)
                link(nc.vector.tensor_copy(e.vec[:, :], e.ps[:, 5, 0:NVEC + NCW]))
                for i in range(2):
                    dve.wait_ge(mod_turned, i + 1)
                    mod_finish(nc, e, link, 0, i, 4, 0)
                    dve.sem_inc(mod_taken, 1)
    end_block(nc)


def sample_view(ap3):
    return ap3.rearrange("p k (b t) -> p k b t", t=DS)


def block_norm(nc, e, xT, hT, l, name, scratch, save=False, loads=None):
    with ExitStack() as ctx:
        rstd = ctx.enter_context(nc.sbuf_tensor(f"{name}_rstd", [P, T], F32))
        ones = ctx.enter_context(nc.sbuf_tensor(f"{name}_ones", [P, P], F32))
        sq = scratch
        squared, summed, root, rooted = (new_sem(nc, f"{name}_{s}") for s in ("squared", "summed", "root_in", "rooted"))
        normed, ones_set = new_sem(nc, f"{name}_normed"), new_sem(nc, f"{name}_ones_set")
        saved = new_sem(nc, f"{name}_x_saved")
        with nc.Block() as block:
            if save:
                @block.sync
                def _(sp):
                    loads(sp)
                    sp.dma_start(e.x_save, xT[:, :, :]).then_inc(saved, 16)
                    sp.wait_ge(saved, 16)

            @block.gpsimd
            def _(pool):
                nc.gpsimd.memset(ones[:, :], 1.0).then_inc(ones_set, 1)

            @block.tensor
            def _(pe):
                pe.wait_ge(ones_set, 1)
                for c, (s, n) in enumerate(CHUNKS):
                    for k in range(KD):
                        if k % 4 == 0:
                            pe.wait_ge(squared, 2 * c + k // 4 + 1)
                        last = mm(nc, e.ps[:, c, 0:n], ones[:, :], sq[:, k, s:s + n], k == 0, k == KD - 1)
                    last.then_inc(summed, 1)

            @block.scalar
            def _(act):
                def squares(c):
                    s, n = CHUNKS[c]
                    for k in (0, 4):
                        nc.scalar.activation(sq[:, k:k + 4, s:s + n], xT[:, k:k + 4, s:s + n], ACT.Square).then_inc(squared, 1)

                squares(0)
                squares(1)
                for c, (s, n) in enumerate(CHUNKS):
                    act.wait_ge(root, c + 1)
                    nc.scalar.activation(rstd[:, s:s + n], rstd[:, s:s + n], ACT.Sqrt).then_inc(rooted, 1)
                    if c == 0:
                        squares(2)
                    t = min(s + n, TP) if l is not None else s + n
                    for k in range(KD):
                        if k % 4 == 0:
                            act.wait_ge(normed, 2 * c + k // 4 + 1)
                        if l is None:
                            w = e.vec[:, VEC["final_w"][0] + k:VEC["final_w"][0] + k + 1]
                            nc.scalar.activation(hT[:, k, s:t], hT[:, k, s:t], ACT.Copy, scale=w)
                        else:
                            nc.scalar.activation(hT[:, k, s:t], hT[:, k, s:t], ACT.Identity,
                                                 scale=e.mod[:, l, 8 + k, 0:1], bias=e.mod[:, l, k, 0:1])

            @block.vector
            def _(dve):
                link = make_link(dve, e.dve_step, e.dve_n)

                def roots(c):
                    s, n = CHUNKS[c]
                    dve.wait_ge(summed, c + 1)
                    link(nc.vector.tensor_scalar(rstd[:, s:s + n], e.ps[:, c, 0:n], 1.0 / D, EPS, ALU.mult, ALU.add))
                    nc.vector.reciprocal(rstd[:, s:s + n], rstd[:, s:s + n]).then_inc(root, 1)

                roots(0)
                for c, (s, n) in enumerate(CHUNKS):
                    dve.wait_ge(rooted, c + 1)
                    for k in (0, 4):
                        nc.vector.tensor_tensor(hT[:, k:k + 4, s:s + n], xT[:, k:k + 4, s:s + n],
                                                rstd[:, None, s:s + n].broadcast_to([P, 4, n]), ALU.mult).then_inc(normed, 1)
                    if c + 1 < len(CHUNKS):
                        roots(c + 1)
                dve.wait_ge(normed, 2 * len(CHUNKS))
                if l is not None:
                    hs = sample_view(hT[:, :, TP:T])
                    link(nc.vector.tensor_tensor(hs, hs, e.mod[:, l, 8:16, 1:9][:, :, :, None].broadcast_to([P, KD, DB, DS]), ALU.mult))
                    nc.vector.tensor_tensor(hs, hs, e.mod[:, l, 0:8, 1:9][:, :, :, None].broadcast_to([P, KD, DB, DS]), ALU.add)
    end_block(nc)






def block_attn_proj(nc, e, hT, A):
    cols = ATTN_COLS
    with ExitStack() as ctx:
        def sb(name, shape, dt=F32):
            return ctx.enter_context(nc.sbuf_tensor(name, shape, dt))
        w, w_in = e.w_attn, e.w_attn_in
        qrot8 = sb("q_rotated_samples", [P, 512])
        rope = sb("rope_table", [P, 2, NT, HD])
        t1, t2 = sb("rope_t1", [P, 2, 512]), sb("rope_t2", [P, 2, 512])
        per = sb("pe_rows", [2 * CB, 2, HD])
        rope_in = new_sem(nc, "rope_in")
        proj_done, q_freed, kv_freed = (new_sem(nc, s) for s in ("attn_proj_done", "q_bank_freed", "kv_bank_freed"))
        rot_mult, rot_done = new_sem(nc, "rope_mult"), new_sem(nc, "rope_done")
        tr_done, tr_act, tr_dve = (new_sem(nc, s) for s in ("attn_transposed", "attn_T_copied_act", "attn_T_copied_dve"))
        rows_out, pe_ready = e.stored["kv_rows"], new_sem(nc, "pe_T_ready")

        def qrot(m):
            return A.cmpT[:, m // 4, TP + (m % 4) * 512:TP + (m % 4 + 1) * 512] if m < NTP else qrot8[:, :]

        def bank_freed(eng, g):
            if g < NT:
                eng.wait_ge(q_freed, g + 1)
            else:
                eng.wait_ge(kv_freed, g - NT + 1)

        with nc.Block() as block:
            @block.sync
            def _(sp):
                sp.dma_start(rope[:, :, :, :], e.k_rope.rearrange("p (a m d) -> p a m d", a=2, m=NT)).then_inc(rope_in, 16)
                sp.dma_start(per[:, 0, :], e.nsa_cmp_pe[0].rearrange("v c d -> (v c) d")).then_inc(rope_in, 16)
                sp.dma_start(per[:, 1, :], e.nsa_cmp_pe[0].rearrange("v c d -> (v c) d")).then_inc(rope_in, 16)
                sp.wait_ge(proj_done, NT)
                load_attn_w(sp, e, w[:, 0], w_in[0], cols[2])
                for b in range(DB):
                    sp.dma_start(e.outs[5][0, b, 0:PAST - DS].rearrange("t a g d -> t (a g d)"),
                                 e.cache_nsa_win[0, b, DS:PAST].rearrange("t a g d -> t (a g d)")).then_inc(rows_out, 16)
                sp.wait_ge(rot_done, 3 * NT)
                sp.wait_ge(kv_freed, 2 * NT)
                kv = A.kvrow
                sp.dma_start(e.outs[2][0, 0].rearrange("(m p) a g d -> p m (a g d)", p=P), kv[:, 0:NTP, 0:512]).then_inc(rows_out, 16)
                sp.dma_start(e.outs[3][0].rearrange("b t a g d -> (b t) (a g d)"), kv[0:TS, NTP, 0:512]).then_inc(rows_out, 16)
                sp.dma_start(e.outs[4][0, 0].rearrange("(m p) a g d -> p m (a g d)", p=P),
                             kv[:, NTP - WIN // P:NTP, 512:768]).then_inc(rows_out, 16)
                for b in range(DB):
                    sp.dma_start(e.outs[5][0, b, PAST - DS:PAST].rearrange("t a g d -> t (a g d)"),
                                 kv[b * DS:(b + 1) * DS, NTP, 512:768]).then_inc(rows_out, 16)
                sp.dma_start(e.g_save, A.gates[0:TS, NTP, :]).then_inc(rows_out, 16)
                sp.wait_ge(rows_out, 16 * (2 * DB + 4))

            @block.tensor
            def _(pe):
                def project(c):
                    s, n = cols[c]
                    pe.wait_ge(w_in[c % 2], 16 * (c // 2 + 1))
                    for m in range(NT):
                        g, r = c * NT + m, rows(m)
                        if g >= 4:
                            bank_freed(pe, g - 4)
                        for k in range(KD):
                            last = mm(nc, e.ps[0:r, g % 4, 0:n], hT[:, k, m * P:m * P + r], w[:, c % 2, k, 0:n], k == 0, k == KD - 1)
                        last.then_inc(proj_done, 1)

                def turn(i, source):
                    if i >= 2:
                        pe.wait_ge(tr_act, i - 1)
                        if i - 2 >= NT:
                            pe.wait_ge(tr_dve, i - 1 - NT)
                    m, r = i % NT, rows(i % NT)
                    for j in range(4):
                        s = source(m, r, j)
                        b, at = (4 + i % 2, j) if i < NT or j < 2 else (6 + i % 2, j - 2)
                        last = nc.tensor.transpose(e.ps[:, b, at * P:at * P + r], s, e.ident[0:r, 0:r])
                    last.then_inc(tr_done, 1)

                pe.wait_ge(rope_in, 48)
                nc.tensor.transpose(e.ps[:, 6, 0:2 * CB], per[:, :, :].rearrange("p a d -> p (a d)"), e.ident[0:2 * CB, 0:2 * CB]).then_inc(pe_ready, 1)
                project(0)
                project(1)
                for m in range(NT):
                    pe.wait_ge(rot_done, m + 1)
                    turn(m, lambda m, r, j: qrot(m)[0:r, j * P:(j + 1) * P])
                project(2)
                for m in range(NT):
                    pe.wait_ge(rot_done, 2 * NT + m + 1)
                    turn(NT + m, lambda m, r, j: A.kvrow[0:r, m, (0, 128, 256, 512)[j]:(128, 256, 384, 640)[j]])

            @block.scalar
            def _(act):
                for m in range(NT):
                    g, r = NT + m, rows(m)
                    act.wait_ge(proj_done, g + 1)
                    nc.scalar.activation(A.gates[0:r, m, :], e.ps[0:r, g % 4, 0:24], ACT.Sigmoid)
                    nc.scalar.copy(A.kvrow[0:r, m, 0:384], e.ps[0:r, g % 4, 24:408]).then_inc(kv_freed, 1)
                for m in range(NT):
                    act.wait_ge(tr_done, m + 1)
                    r = rows(m)
                    nc.scalar.copy(A.QT[:, :, m * P:m * P + r], e.ps[:, 4 + m % 2, :].rearrange("p (j t) -> p j t", j=4)[:, :, 0:r]).then_inc(tr_act, 1)
                for m in range(NT):
                    g, r = 2 * NT + m, rows(m)
                    act.wait_ge(proj_done, g + 1)
                    nc.scalar.copy(A.kvrow[0:r, m, 384:768], e.ps[0:r, g % 4, 0:384]).then_inc(kv_freed, 1)
                for m in range(NT):
                    i, r = NT + m, rows(m)
                    act.wait_ge(tr_done, i + 1)
                    at = m * P if m < NTP else NKEY
                    nc.scalar.copy(A.KT[:, :, at:at + r], e.ps[:, 6 + i % 2, 0:256].rearrange("p (j t) -> p j t", j=2)[:, :, 0:r]).then_inc(tr_act, 1)

            @block.vector
            def _(dve):
                n = [0]

                def rotate(src, m, heads):
                    i, r = n[0], rows(m)
                    if i >= 2:
                        dve.wait_ge(rot_done, i - 1)
                    a, b = heads
                    shape = [r, a, b, HD]
                    v1 = t1[0:r, i % 2, 0:a * b * HD].rearrange("p (a b d) -> p a b d", a=a, b=b)
                    v2 = t2[0:r, i % 2, 0:a * b * HD].rearrange("p (a b d) -> p a b d", a=a, b=b)
                    cos = rope[0:r, 0, m, :][:, None, None, :].broadcast_to(shape)
                    sin = rope[0:r, 1, m, :][:, None, None, :].broadcast_to(shape)
                    nc.vector.tensor_tensor(v1, src, cos, ALU.mult)
                    nc.vector.tensor_tensor(v2[:, :, :, 0:32], src[:, :, :, 32:64], sin[:, :, :, 0:32], ALU.mult)
                    last = nc.vector.tensor_tensor(v2[:, :, :, 32:64], src[:, :, :, 0:32], sin[:, :, :, 32:64], ALU.mult)
                    n[0] += 1
                    last.then_inc(rot_mult, 1)
                    return last

                link = make_link(dve, e.dve_step, e.dve_n)
                dve.wait_ge(rope_in, 48)
                dve.wait_ge(pe_ready, 1)
                link(nc.vector.tensor_copy(A.peT[:, :], e.ps[:, 6, 0:2 * CB]))
                for m in range(NT):
                    dve.wait_ge(proj_done, m + 1)
                    rotate(e.ps[0:rows(m), m % 4, :].rearrange("p (g a d) -> p g a d", g=G, a=HG), m, (G, HG))
                    dve.wait_ge(rot_mult, m + 1)
                    dve.sem_inc(q_freed, 1)
                for m in range(NT):
                    dve.wait_ge(kv_freed, m + 1)
                    v = A.kvrow[0:rows(m), m, 0:512].rearrange("p (a x) -> p a x", a=2)[:, :, 0:128].rearrange("p a (b d) -> p a b d", b=2)
                    rotate(v, m, (2, 2))
                for m in range(NT):
                    dve.wait_ge(kv_freed, NT + m + 1)
                    rotate(A.kvrow[0:rows(m), m, 512:640].rearrange("p (a b d) -> p a b d", a=1, b=2), m, (1, 2))
                for m in range(NTP):
                    i = NT + m
                    dve.wait_ge(tr_done, i + 1)
                    out = A.cmpT[:, :, m * P:(m + 1) * P].rearrange("p v (n c) -> p v n c", c=CB)
                    src = e.ps[:, 4 + i % 2, 0:256].rearrange("p (v n c) -> p v n c", v=2, c=CB)
                    nc.vector.tensor_tensor(out, src, A.peT[:, :].rearrange("p (v c) -> p v c", v=2)[:, :, None, :].broadcast_to([P, 2, 4, CB]),
                                            ALU.add).then_inc(tr_dve, 1)

            @block.gpsimd
            def _(pool):
                for i in range(3 * NT):
                    m, r = i % NT, rows(i % NT)
                    pool.wait_ge(rot_mult, i + 1)
                    if i < NT:
                        out = qrot(m)[0:r, :].rearrange("p (a g d) -> p g a d", a=HG, g=G)
                        a, b = G, HG
                    elif i < 2 * NT:
                        out = A.kvrow[0:r, m, 0:512].rearrange("p (a x) -> p a x", a=2)[:, :, 0:128].rearrange("p a (b d) -> p a b d", b=2)
                        a, b = 2, 2
                    else:
                        out = A.kvrow[0:r, m, 512:640].rearrange("p (a b d) -> p a b d", a=1, b=2)
                        a, b = 1, 2
                    v1 = t1[0:r, i % 2, 0:a * b * HD].rearrange("p (a b d) -> p a b d", a=a, b=b)
                    v2 = t2[0:r, i % 2, 0:a * b * HD].rearrange("p (a b d) -> p a b d", a=a, b=b)
                    nc.gpsimd.tensor_tensor(out, v1, v2, ALU.add).then_inc(rot_done, 1)
    end_block(nc)


def block_past(nc, e, A):
    NP = DB * NPG
    with ExitStack() as ctx:
        def sb(name, shape, dt=F32):
            return ctx.enter_context(nc.sbuf_tensor(name, shape, dt))
        page = sb("page_rows", [P, 4, 768])
        w1, w2 = sb("cmp_w1", [P, 2, CB // 2, 2 * HD]), sb("cmp_w2", [P, 2, HD])
        hid = sb("cmp_hidden", [P, 2, G, NKEY // CB])
        pt = sb("page_numbers", [1, NP], I32)
        pt_in, w2_in = new_sem(nc, "page_table_in"), new_sem(nc, "cmp_w2_in")
        w1_in, w1_used = [new_sem(nc, f"cmp_w1_in{i}") for i in range(2)], new_sem(nc, "cmp_w1_used")
        page_in = [new_sem(nc, f"page_in{i}") for i in range(4)]
        vpast_in = new_sem(nc, "v_past_in")
        tr_done, tr_act, tr_dve = (new_sem(nc, s) for s in ("page_transposed", "page_T_copied_act", "page_T_copied_dve"))
        hid_ready, cmp_done, zeroed = (new_sem(nc, s) for s in ("cmp_hidden_ready", "cmp_done", "v_cmp_zeroed"))
        with nc.Block() as block:
            @block.sync
            def _(sp):
                def load_w1(n):
                    w1v = e.nsa_cmp_w1[0, n // 2].rearrange("(c d) h -> d c h", d=HD)[:, (n % 2) * CB // 2:(n % 2 + 1) * CB // 2, :]
                    for g in range(G):
                        sp.dma_start(w1[g * HD:(g + 1) * HD, n % 2], w1v).then_inc(w1_in[n % 2], 16)

                sp.dma_start(pt[:, :], e.page_table.rearrange("b n -> (b n)").rearrange("(a n) -> a n", a=1)).then_inc(pt_in, 16)
                sp.wait_ge(pt_in, 16)
                for i in range(NP):
                    if i >= 4:
                        sp.wait_ge(tr_done, i - 3)
                    number = sp.value_load(pt[0:1, i:i + 1], min_val=0, max_val=NPOOL - 1)
                    src = e.cache_nsa[0][bass.ds(number, 1), :, :, :, :].rearrange("n t a g d -> (n t) (a g d)")
                    sp.dma_start(page[:, i % 4, 0:512], src).then_inc(page_in[i % 4], 16)
                    sp.dma_start(A.vpast[:, i, 0:128], src[:, 384:512]).then_inc(vpast_in, 16)
                    sp.dma_start(page[:, i % 4, 512:768], e.cache_nsa_win[0, i // NPG, (i % NPG) * PAGE:(i % NPG + 1) * PAGE]
                                 .rearrange("t a g d -> t (a g d)")).then_inc(page_in[i % 4], 16)
                    if i == 0:
                        load_w1(0)
                        load_w1(1)
                        sp.dma_start(w2[:, :, :], e.nsa_cmp_w2[0].rearrange("v h d -> h v d")).then_inc(w2_in, 16)
                sp.dma_start(A.vpast[:, :, 128:256], e.cache_nsa_win[0].rearrange("b (n p) a g d -> p (b n) a (g d)", p=P)[:, :, 1, :]).then_inc(vpast_in, 16)
                for n in range(2, 4):
                    sp.wait_ge(w1_used, n - 1)
                    load_w1(n)
                sp.wait_ge(vpast_in, 16 * (NP + 1))

            @block.tensor
            def _(pe):
                for i in range(NP):
                    pe.wait_ge(page_in[i % 4], 32 * (i // 4 + 1))
                    if i >= 2:
                        pe.wait_ge(tr_act, i - 1)
                        pe.wait_ge(tr_dve, i - 1)
                    for j in range(4):
                        s = (0, 128, 256, 512)[j]
                        at = j % 2 * P
                        last = nc.tensor.transpose(e.ps[:, i % 2 + 2 * (j // 2), at:at + P], page[:, i % 4, s:s + P], e.ident)
                    last.then_inc(tr_done, 1)
                pe.wait_ge(tr_dve, NP)
                pe.wait_ge(tr_act, NP)
                for v in range(2):
                    for c in range(CB):
                        n = 2 * v + c // 16
                        if c % 16 == 0:
                            pe.wait_ge(w1_in[n % 2], 32 * (n // 2 + 1))
                        for g in range(G):
                            last = mm(nc, e.ps[:, 2 + 2 * v + g, 0:NKEY // CB], w1[g * HD:(g + 1) * HD, n % 2, c % 16, :],
                                      A.cmpT[g * HD:(g + 1) * HD, v, c:NKEY:CB], c == 0, c == CB - 1)
                        if c % 16 == 15:
                            last.then_inc(w1_used, 1)
                pe.wait_ge(w2_in, 16)
                pe.wait_ge(hid_ready, 2)
                for g in range(G):
                    mm(nc, e.ps[g * HD:(g + 1) * HD, 6, 0:NKEY // CB], w2[:, 0, :], hid[:, 0, g, :], True, True)
                for g in range(G):
                    for h in range(HG):
                        mm(nc, e.ps[h * 32:(h + 1) * 32, 7, g * HD:(g + 1) * HD], hid[:, 1, g, 0:NCP], w2[:, 1, :], True, True)
                for b in range(DB):
                    for g in range(G):
                        at = (b % 4) * P + g * HD
                        last = mm(nc, e.ps[0:NCS, b // 4, at:at + HD], hid[:, 1, g, NCP + b * NCS:NCP + (b + 1) * NCS], w2[:, 1, :], True, True)
                last.then_inc(cmp_done, 1)

            @block.scalar
            def _(act):
                for i in range(NP):
                    act.wait_ge(tr_done, i + 1)
                    nc.scalar.copy(A.KT[:, :, TP + i * P:TP + (i + 1) * P], e.ps[:, 2 + i % 2, 0:256].rearrange("p (j t) -> p j t", j=2)).then_inc(tr_act, 1)
                for v in range(2):
                    act.wait_ge(w1_used, 2 * (v + 1))
                    nc.scalar.activation(hid[:, v, :, :], e.ps[:, 2 + 2 * v:4 + 2 * v, 0:NKEY // CB], ACT.Silu).then_inc(hid_ready, 1)

            @block.gpsimd
            def _(pool):
                nc.gpsimd.memset(A.vcd[:, :, :], 0.0).then_inc(zeroed, 1)

            @block.vector
            def _(dve):
                for i in range(NP):
                    dve.wait_ge(tr_done, i + 1)
                    out = A.cmpT[:, :, TP + i * P:TP + (i + 1) * P].rearrange("p v (n c) -> p v n c", c=CB)
                    src = e.ps[:, i % 2, 0:256].rearrange("p (v n c) -> p v n c", v=2, c=CB)
                    nc.vector.tensor_tensor(out, src, A.peT[:, :].rearrange("p (v c) -> p v c", v=2)[:, :, None, :].broadcast_to([P, 2, 4, CB]),
                                            ALU.add).then_inc(tr_dve, 1)
                dve.wait_ge(cmp_done, 1)
                dve.wait_ge(zeroed, 1)
                nc.vector.tensor_copy(A.kccT[:, :], e.ps[:, 6, 0:NKEY // CB])
                for h in range(HG):
                    nc.vector.tensor_copy(A.vcd[h * 32:(h + 1) * 32, :, h * HD:(h + 1) * HD],
                                          e.ps[h * 32:(h + 1) * 32, 7, 0:128].rearrange("p (g d) -> p g d", g=G))
                nc.vector.tensor_copy(A.vcs[:, 0:4, :], e.ps[0:NCS, 0, :].rearrange("p (b d) -> p b d", b=4))
                nc.vector.tensor_copy(A.vcs[:, 4:8, :], e.ps[0:NCS, 1, :].rearrange("p (b d) -> p b d", b=4))
    end_block(nc)




def block_attn_samples(nc, e, A):
    NK = PAST + TS
    with ExitStack() as ctx:
        def sb(name, shape, dt=F32):
            return ctx.enter_context(nc.sbuf_tensor(name, shape, dt))
        QS = sb("q_block_diagonal", [P, DB, G, HG * DS])
        p, pc = sb("p_samples", [P, 2, 2, NK]), sb("p_cmp_samples", [P, 2, NCS])
        pT, pcT = sb("p_T_samples", [P, 2, 2, 384]), sb("p_cmp_T_samples", [NCS, 2, P])
        mx, neg, den = sb("row_max_samples", [P, 2, 3]), sb("neg_max_samples", [P, 2, 3]), sb("den_samples", [P, 2, 3])
        grow, coef = sb("gate_rows", [P, 2, 3]), sb("coef_samples", [P, 2, 3, G])
        acc = sb("acc_samples", [P, 2, HD])
        zeroed, q_ready, s_done, neg_ready, p_ready = (new_sem(nc, "smp_" + s) for s in ("q_zeroed", "q_ready", "scores", "neg_max", "p_ready"))
        pt_done, pt_ready, o_done, acc_done, g_in, o_out = (new_sem(nc, "smp_" + s) for s in ("p_turned", "p_T_ready", "o_done", "acc", "gates_in", "o_saved"))
        with nc.Block() as block:
            @block.sync
            def _(sp):
                sp.dma_start(A.w_za[:, :, :], e.w_in_even[0, :, E_ZA:E_ZB].rearrange("(k p) n -> p k n", p=P)).then_inc(A.w_za_in, 16)
                for f in range(2):
                    for br in range(3):
                        for b in range(4):
                            src = e.g_save.rearrange("(b t) (a h) -> b a h t", t=DS, a=3)[4 * f + b, br].rearrange("h (t x) -> h t x", x=1)
                            sp.dma_start(grow[32 * b:32 * (b + 1), f, br:br + 1], src, allow_slow_non_contiguous=True).then_inc(g_in, 16)
                for f in range(2):
                    sp.wait_ge(acc_done, f + 1)
                    for b in range(4):
                        dst = e.o_save.rearrange("(b t) (h d) -> b h t d", t=DS, d=HD)[4 * f + b]
                        sp.dma_start(dst, acc[32 * b:32 * (b + 1), f, :]).then_inc(o_out, 16)
                sp.wait_ge(o_out, 16 * DB)
                sp.dma_start(A.o_smp[:, :], e.o_save).then_inc(o_out, 16)
                sp.wait_ge(o_out, 16 * (DB + 1))

            @block.gpsimd
            def _(pool):
                nc.gpsimd.memset(QS[:, :, :, :], 0.0).then_inc(zeroed, 1)

            @block.tensor
            def _(pe):
                pe.wait_ge(q_ready, 1)
                for f in range(2):
                    lrows = QS[:, 4 * f:4 * f + 4, :, :].rearrange("p b g r -> p (b g r)")
                    for br in range(2):
                        for b in range(4):
                            at = TP + (4 * f + b) * PAST
                            mm(nc, e.ps[32 * b:32 * (b + 1), 4 * f + br, 0:PAST], lrows[:, 32 * b:32 * (b + 1)], A.KT[:, br, at:at + PAST], True, True)
                        mm(nc, e.ps[:, 4 * f + br, PAST:NK], lrows, A.KT[:, br, NKEY:NKEY + TS], True, False)
                        last = mm(nc, e.ps[:, 4 * f + br, PAST:NK], e.identb, e.B["new"][:, f * TS:(f + 1) * TS], False, True)
                    for b in range(4):
                        at = NCP + (4 * f + b) * NCS
                        last = mm(nc, e.ps[32 * b:32 * (b + 1), 4 * f, NK:NK + NCS], lrows[:, 32 * b:32 * (b + 1)], A.kccT[:, at:at + NCS], True, True)
                    last.then_inc(s_done, 1)
                for f in range(2):
                    pe.wait_ge(p_ready, f + 1)
                    for br in range(2):
                        for j, (s, n) in enumerate(((0, P), (P, P), (PAST, TS))):
                            nc.tensor.transpose(e.ps[0:n, 4 * f + 2 + br, j * P:(j + 1) * P], p[:, f, br, s:s + n], e.ident)
                    nc.tensor.transpose(e.ps[0:NCS, 4 * f + 2, 384:512], pc[:, f, :], e.ident).then_inc(pt_done, 1)
                for f in range(2):
                    pe.wait_ge(pt_ready, f + 1)
                    for b in range(4):
                        mm(nc, e.ps[32 * b:32 * (b + 1), 4 * f + 1, 0:P], pcT[:, f, 32 * b:32 * (b + 1)], A.vcs[:, 4 * f + b, :], True, True)
                    for br in range(2):
                        out = e.ps[:, 4 * f + 1, (br + 1) * P:(br + 2) * P]
                        mm(nc, out, pT[0:TS, f, br, PAST:384], A.kvrow[0:TS, NTP, (384, 640)[br]:(512, 768)[br]], True, False)
                        for b in range(4):
                            for n in range(NPG):
                                last = mm(nc, out[32 * b:32 * (b + 1)], pT[:, f, br, n * P + 32 * b:n * P + 32 * (b + 1)],
                                          A.vpast[:, (4 * f + b) * NPG + n, br * P:(br + 1) * P], False, n == NPG - 1)
                    last.then_inc(o_done, 1)

            @block.scalar
            def _(act):
                for f in range(2):
                    act.wait_ge(neg_ready, f + 1)
                    for br in range(2):
                        nc.scalar.activation(p[:, f, br, :], e.ps[:, 4 * f + br, 0:NK], ACT.Exp, bias=neg[:, f, br + 1:br + 2], scale=SCALE,
                                             accum_out=den[:, f, br + 1:br + 2])
                    nc.scalar.activation(pc[:, f, :], e.ps[:, 4 * f, NK:NK + NCS], ACT.Exp, bias=neg[:, f, 0:1], scale=SCALE,
                                         accum_out=den[:, f, 0:1]).then_inc(p_ready, 1)

            @block.vector
            def _(dve):
                link = make_link(dve, e.dve_step, e.dve_n)
                dve.wait_ge(zeroed, 1)
                for g in range(G):
                    last = nc.vector.tensor_copy(QS[g * HD:(g + 1) * HD, :, g, :].rearrange("p b (h t) -> p b h t", t=DS),
                                                 A.QT[g * HD:(g + 1) * HD, :, TP:T].rearrange("p h (b t) -> p b h t", t=DS))
                last.then_inc(q_ready, 1)
                for f in range(2):
                    dve.wait_ge(s_done, f + 1)
                    nc.vector.tensor_reduce(mx[:, f, 0:1], e.ps[:, 4 * f, NK:NK + NCS], AX.X, ALU.max)
                    nc.vector.tensor_reduce(mx[:, f, 1:2], e.ps[:, 4 * f, 0:NK], AX.X, ALU.max)
                    link(nc.vector.tensor_reduce(mx[:, f, 2:3], e.ps[:, 4 * f + 1, 0:NK], AX.X, ALU.max))
                    nc.vector.tensor_scalar(neg[:, f, :], mx[:, f, :], -SCALE, None, ALU.mult).then_inc(neg_ready, 1)
                for f in range(2):
                    dve.wait_ge(pt_done, f + 1)
                    for br in range(2):
                        nc.vector.tensor_copy(pT[:, f, br, 0:PAST], e.ps[:, 4 * f + 2 + br, 0:PAST])
                        nc.vector.tensor_copy(pT[0:TS, f, br, PAST:384], e.ps[0:TS, 4 * f + 2 + br, PAST:384])
                    nc.vector.tensor_copy(pcT[:, f, :], e.ps[0:NCS, 4 * f + 2, 384:512]).then_inc(pt_ready, 1)
                dve.wait_ge(g_in, 16 * 24)
                link(nc.vector.reciprocal(den[:, :, :], den[:, :, :]))
                link(nc.vector.tensor_tensor(den[:, :, :], den[:, :, :], grow[:, :, :], ALU.mult))
                for f in range(2):
                    for g in range(G):
                        last = nc.vector.tensor_scalar(coef[:, f, :, g], den[:, f, :], e.F["own"][:, g:g + 1], None, ALU.mult)
                link(last)
                for f in range(2):
                    dve.wait_ge(o_done, f + 1)
                    for i in range(3 * G):
                        br, g = i // G, i % G
                        o = e.ps[:, 4 * f + 1, br * P + g * HD:br * P + (g + 1) * HD]
                        if i == 0:
                            last = nc.vector.tensor_scalar(acc[:, f, :], o, coef[:, f, br, g:g + 1], None, ALU.mult)
                        else:
                            last = nc.vector.scalar_tensor_tensor(acc[:, f, :], o, coef[:, f, br, g:g + 1], acc[:, f, :], ALU.mult, ALU.add)
                        if i < 3 * G - 1:
                            link(last)
                    last.then_inc(acc_done, 1)
    end_block(nc)


def attention_items():
    items = []
    for i in range(NT):
        items.append(("z", i, 0, 0))
        if i < NTP:
            items.append(("cmp", i, 0, 0))
        heads = [("att", i, h, br) for h in range(H) for br in range(2)] if i < NTP else []
        items += heads[:2]
        if i:
            items.append(("fin", i - 1, 0, 0))
        items += heads[2:]
    items.append(("fin", NT - 1, 0, 0))
    return items


def block_attn_prompt(nc, e, A):
    items = attention_items()
    with ExitStack() as ctx:
        def sb(name, shape, dt=F32):
            return ctx.enter_context(nc.sbuf_tensor(name, shape, dt))
        w = A.w_za
        p, pT = sb("p_att", [P, 2, 1024]), sb("p_T_att", [P, 4, 512])
        qz = sb("q_T_zeroed", [P, 2, G, HG * P])
        zs, acc, tmp = sb("silu_z_a", [P, 2, 512]), sb("acc_att", [P, 2, 512]), sb("tmp_att", [P, 2, 2, 512])
        mx, neg = sb("row_max_att", [P, 4, 8]), sb("neg_max_att", [P, 4])
        den, coef = sb("den_att", [P, 2, 3, H]), sb("coef_att", [P, 2, 3, H])
        names = ("scores", "neg_ready", "p_ready", "turned", "pT_ready_dve", "pT_ready_act", "pv_done", "cmp_taken", "o_scaled", "acc_ready")
        s_done, neg_ready, p_ready, t_done, pt_dve, pt_act, pv_done, cmp_taken, o_scaled, acc_ready = \
            (new_sem(nc, "att_" + s) for s in names)
        qz_zeroed, q_ready = new_sem(nc, "att_q_zeroed"), new_sem(nc, "att_q_ready")
        plan, s, a, g, v, c = [], 0, 0, 0, 0, 0
        for kind, i, h, br in items:
            lo = max(0, i - WIN // P) if br else 0
            blocks = {"z": 0, "cmp": 2, "fin": 4, "att": i + 1 - lo}[kind]
            plan.append((s, a, g, v, lo, blocks))
            s += kind != "fin"
            a += kind in ("cmp", "att")
            g += -(-blocks // 4)
            v += kind in ("cmp", "att")
        groups = lambda n: [(plan[n][2] + x, 4 * x, min(4, plan[n][5] - 4 * x)) for x in range(-(-plan[n][5] // 4))]

        def wait_turned_copied(eng, g):
            eng.wait_ge((pt_dve, pt_act)[g % 2], g // 2 + 1)

        def wait_scores_taken(eng, s):
            eng.wait_ge(p_ready, s + 1)

        def copy_group(eng, copy, n, parity, sem):
            kind, i, h, br = items[n]
            for g, b0, nb in groups(n):
                if g % 2 != parity:
                    continue
                eng.wait_ge(t_done, g + 1)
                if kind == "fin":
                    r = rows(i)
                    src = e.ps[:, 4 + g % 2, :].rearrange("p (j t) -> p j t", j=4)[:, :, 0:r]
                    copy(A.oT[:, :, i * P:i * P + r], src).then_inc(sem, 1)
                else:
                    copy(pT[:, g % 4, 0:nb * P], e.ps[:, 4 + g % 2, 0:nb * P]).then_inc(sem, 1)

        with nc.Block() as block:
            @block.tensor
            def _(pe):
                def scores(n):
                    kind, i, h, br = items[n]
                    s, _, _, _, lo, blocks = plan[n]
                    if kind == "fin":
                        return
                    if s >= 2:
                        wait_scores_taken(pe, s - 2)
                    r, two = rows(i), 2 * (s % 2)
                    if kind == "z":
                        if i == 0:
                            pe.wait_ge(A.w_za_in, 16)
                        for k in range(KD):
                            last = mm(nc, e.ps[0:r, two, :], A.hT[:, k, i * P:i * P + r], w[:, k, :], k == 0, k == KD - 1)
                    elif kind == "cmp":
                        pe.wait_ge(q_ready, i + 1)
                        for h in range(H):
                            g = h // HG
                            mm(nc, e.ps[:, two + g, (h % HG) * NCP:(h % HG + 1) * NCP], qz[:, i % 2, g, (h % HG) * P:(h % HG + 1) * P],
                               A.kccT[:, 0:NCP], h % HG == 0, False)
                        mask = e.B["cmp"][:, i * NCP:(i + 1) * NCP][:, None, :].broadcast_to([P, HG, NCP])
                        for g in range(G):
                            last = mm(nc, e.ps[:, two + g, 0:HG * NCP].rearrange("p (h n) -> p h n", h=HG), e.identb, mask, False, True)
                    else:
                        g = h // HG
                        q = qz[:, i % 2, g, (h % HG) * P:(h % HG + 1) * P]
                        for c in range(-(-blocks // 4)):
                            nb = min(4, blocks - 4 * c)
                            at = (lo + 4 * c) * P
                            mm(nc, e.ps[:, two + c, 0:nb * P], q, A.KT[:, br, at:at + nb * P], True, False)
                            if c == 0 and br and i >= WIN // P:
                                mm(nc, e.ps[:, two, 0:P], e.identb, e.B["old"], False, False)
                        last = mm(nc, e.ps[:, two + c, (nb - 1) * P:nb * P], e.identb, e.B["causal"], False, True)
                    last.then_inc(s_done, 1)

                def turn(n):
                    kind, i, h, br = items[n]
                    s = plan[n][0]
                    if kind == "z":
                        return
                    if kind == "fin":
                        pe.wait_ge(acc_ready, i + 1)
                    else:
                        wait_scores_taken(pe, s)
                    r = rows(i)
                    for g, b0, nb in groups(n):
                        if g >= 2:
                            wait_turned_copied(pe, g - 2)
                        for j in range(nb):
                            src = acc[0:r, i % 2, j * P:(j + 1) * P] if kind == "fin" else p[:, s % 2, (b0 + j) * P:(b0 + j + 1) * P]
                            last = nc.tensor.transpose(e.ps[:, 4 + g % 2, j * P:j * P + r], src, e.ident[0:r, 0:r])
                        last.then_inc(t_done, 1)

                def values(n):
                    kind, i, h, br = items[n]
                    _, _, _, v, lo, blocks = plan[n]
                    if kind in ("z", "fin"):
                        return
                    if kind == "cmp" and i:
                        pe.wait_ge(o_scaled, i)
                    if kind == "att" and h == 0 and br == 0:
                        pe.wait_ge(cmp_taken, i + 1)
                    for g, b0, nb in groups(n):
                        wait_turned_copied(pe, g)
                        for j in range(nb):
                            pt = pT[:, g % 4, j * P:(j + 1) * P]
                            if kind == "cmp":
                                last = mm(nc, e.ps[:, 6, j * 256:(j + 1) * 256], pt, A.vcd[:, j, :], True, True)
                            else:
                                at = (384, 640)[br] + (h // HG) * HD
                                last = mm(nc, e.ps[:, 6 + br, h * HD:(h + 1) * HD], pt, A.kvrow[:, lo + b0 + j, at:at + HD],
                                          b0 + j == 0, b0 + j == blocks - 1)
                    last.then_inc(pv_done, 1)

                scores(0)
                scores(1)
                for n in range(len(items)):
                    turn(n)
                    if n + 2 < len(items):
                        scores(n + 2)
                    if n:
                        values(n - 1)

            @block.scalar
            def _(act):
                def exps(n):
                    kind, i, h, br = items[n]
                    s, a, _, _, _, blocks = plan[n]
                    if kind == "fin":
                        return
                    two, r = 2 * (s % 2), rows(i)
                    if kind == "z":
                        act.wait_ge(s_done, s + 1)
                        if i >= 2:
                            act.wait_ge(acc_ready, i - 1)
                        nc.scalar.activation(zs[0:r, i % 2, :], e.ps[0:r, two, :], ACT.Silu).then_inc(p_ready, 1)
                        return
                    act.wait_ge(neg_ready, a + 1)
                    if kind == "cmp":
                        nc.scalar.activation(p[:, s % 2, 0:H * NCP], p[:, s % 2, 0:H * NCP], ACT.Exp, scale=SCALE).then_inc(p_ready, 1)
                    else:
                        src = e.ps[:, two:two + 2, :].rearrange("p b n -> p (b n)")[:, 0:blocks * P]
                        nc.scalar.activation(p[:, s % 2, 0:blocks * P], src, ACT.Exp, bias=neg[:, a % 4:a % 4 + 1], scale=SCALE,
                                             accum_out=den[:, i % 2, br + 1, h:h + 1]).then_inc(p_ready, 1)

                for n in range(len(items) + 1):
                    if n < len(items):
                        exps(n)
                    if n:
                        copy_group(act, nc.scalar.copy, n - 1, 1, pt_act)

            @block.gpsimd
            def _(pool):
                link = make_link(pool, e.pool_step, e.pool_n)

                def queries(i):
                    for g in range(G):
                        half = slice(g * HD, (g + 1) * HD)
                        link(nc.gpsimd.tensor_copy(qz[half, i % 2, g, :].rearrange("p (h t) -> p h t", h=HG), A.QT[half, :, i * P:(i + 1) * P]))
                    pool.sem_inc(q_ready, 1)

                nc.gpsimd.memset(qz[:, :, :, :], 0.0).then_inc(qz_zeroed, 1)
                pool.wait_ge(qz_zeroed, 1)
                queries(0)
                queries(1)
                for i in range(NT):
                    r = rows(i)
                    o = acc[0:r, i % 2, :]
                    if i < NTP:
                        pool.wait_ge(o_scaled, i + 1)
                        if i + 2 < NTP:
                            pool.wait_ge(s_done, plan[items.index(("att", i, H - 1, 1))][0] + 1)
                            queries(i + 2)
                        link(nc.gpsimd.tensor_tensor(o, o, tmp[:, i % 2, 0, :], ALU.add))
                        link(nc.gpsimd.tensor_tensor(o, o, tmp[:, i % 2, 1, :], ALU.add))
                        nc.gpsimd.tensor_tensor(o, o, zs[0:r, i % 2, :], ALU.mult).then_inc(acc_ready, 1)
                    else:
                        pool.wait_ge(p_ready, plan[[x[:2] for x in items].index(("z", i))][0] + 1)
                        pool.wait_ge(t_done, plan[items.index(("fin", i - 2, 0, 0))][2] + 1)
                        nc.gpsimd.tensor_tensor(o, A.o_smp[:, :], zs[0:r, i % 2, :], ALU.mult).then_inc(acc_ready, 1)

            @block.vector
            def _(dve):
                link = make_link(dve, e.dve_step, e.dve_n)

                def maxima(n):
                    kind, i, h, br = items[n]
                    s, a, _, _, _, blocks = plan[n]
                    if kind in ("z", "fin"):
                        return
                    two = 2 * (s % 2)
                    dve.wait_ge(s_done, s + 1)
                    if kind == "cmp":
                        sc = e.ps[:, two:two + 2, 0:HG * NCP].rearrange("p g (h n) -> p g h n", h=HG)
                        top = mx[:, a % 4, :].rearrange("p (g h) -> p g h", g=G)
                        link(nc.vector.tensor_reduce(top, sc, AX.X, ALU.max))
                        nc.vector.tensor_tensor(p[:, s % 2, 0:H * NCP].rearrange("p (g h n) -> p g h n", g=G, h=HG), sc,
                                                top[:, :, :, None].broadcast_to([P, G, HG, NCP]), ALU.subtract).then_inc(neg_ready, 1)
                    else:
                        src = e.ps[:, two:two + 2, :].rearrange("p b n -> p (b n)")[:, 0:blocks * P]
                        link(nc.vector.tensor_reduce(mx[:, a % 4, 0:1], src, AX.X, ALU.max))
                        nc.vector.tensor_scalar(neg[:, a % 4:a % 4 + 1], mx[:, a % 4, 0:1], -SCALE, None, ALU.mult).then_inc(neg_ready, 1)

                def cmp_sums(n):
                    _, i, _, _ = items[n]
                    s = plan[n][0]
                    gates = A.gates[:, i, 0:H]
                    c = coef[:, i % 2, 0, :]
                    dve.wait_ge(p_ready, s + 1)
                    link(nc.vector.tensor_reduce(c, p[:, s % 2, 0:H * NCP].rearrange("p (h n) -> p h n", h=H), AX.X, ALU.add))
                    link(nc.vector.reciprocal(c, c))
                    link(nc.vector.tensor_tensor(c, c, gates, ALU.mult))
                    if i == 0:
                        link(nc.vector.tensor_scalar(c, c, e.F["valid"], None, ALU.mult))

                def cmp_scaled(n):
                    _, i, _, _ = items[n]
                    v = plan[n][3]
                    c = coef[:, i % 2, 0, :]
                    dve.wait_ge(pv_done, v + 1)
                    if i >= 2:
                        dve.wait_ge(t_done, plan[items.index(("fin", i - 2, 0, 0))][2] + 1)
                    nc.vector.tensor_tensor(acc[:, i % 2, :].rearrange("p (h d) -> p h d", h=H), e.ps[:, 6, :].rearrange("p (h d) -> p h d", h=H),
                                            c[:, :, None].broadcast_to([P, H, HD]), ALU.mult).then_inc(cmp_taken, 1)

                def tile_sums(n):
                    _, i, _, _ = items[n]
                    s, _, _, v, _, _ = plan[n]
                    c = coef[:, i % 2, 1:3, :]
                    link(nc.vector.reciprocal(c, den[:, i % 2, 1:3, :]))
                    link(nc.vector.tensor_tensor(c, c, A.gates[:, i, H:3 * H].rearrange("p (a h) -> p a h", a=2), ALU.mult))
                    dve.wait_ge(pv_done, v + 1)
                    if i >= 2:
                        dve.wait_ge(acc_ready, i - 1)
                    for br in range(2):
                        last = nc.vector.tensor_tensor(tmp[:, i % 2, br, :].rearrange("p (h d) -> p h d", h=H), e.ps[:, 6 + br, :].rearrange("p (h d) -> p h d", h=H),
                                                       c[:, br, :][:, :, None].broadcast_to([P, H, HD]), ALU.mult)
                    last.then_inc(o_scaled, 1)

                for n in range(len(items) + 1):
                    if n < len(items):
                        maxima(n)
                    if n:
                        copy_group(dve, nc.vector.tensor_copy, n - 1, 0, pt_dve)
                        if items[n - 1][0] == "cmp":
                            cmp_sums(n - 1)
                    if n >= 2:
                        if items[n - 2][0] == "cmp":
                            cmp_scaled(n - 2)
                        if items[n - 2][0] == "att" and items[n - 2][2:] == (H - 1, 1):
                            tile_sums(n - 2)
    end_block(nc)




def block_ssd_proj(nc, e, hT, S):
    NG = KC * 3
    with ExitStack() as ctx:
        def sb(name, shape, dt=F32):
            return ctx.enter_context(nc.sbuf_tensor(name, shape, dt))
        w, wdt = sb("w_xbc", [P, 2, KD, 256]), sb("w_dt", [P, KD, SH])
        raw, raws, acc = sb("xbc_raw", [P, 2, 3 + TP]), sb("xbc_raw_samples", [P, 2, DB, 3 + DS]), sb("conv_acc", [P, 2, T])
        prow, prevT = sb("conv_state_rows", [DB * 3, CCH]), sb("conv_state_T", [P, KC, DB * 3])
        cv, cvrow = sb("conv_last", [P, KC, 27]), sb("conv_last_rows", [27, CCH])
        x1, x2, x3 = (sb(f"softplus_{i}", [P, NT, SH]) for i in range(3))
        w_in, dt_in, prev_in = [new_sem(nc, f"w_xbc_in{i}") for i in range(2)], new_sem(nc, "w_dt_in"), new_sem(nc, "conv_state_in")
        names = ("zeroed", "prev_done", "prev_ready", "proj_done", "raw_ready", "prev_put", "conv_done", "act_done", "kept", "cv_turned", "cv_copied", "dt_done", "abs_ready", "dt_act")
        zeroed, prev_done, prev_ready, proj_done, raw_ready, prev_put, conv_done, act_done, kept, cv_turned, cv_copied, dt_done, abs_ready, dt_act = \
            (new_sem(nc, "conv_" + s) for s in names)
        out = e.stored["conv"]
        with nc.Block() as block:
            @block.sync
            def _(sp):
                sp.dma_start(prow[:, :], e.state_ssd_conv[0].rearrange("b t c -> (b t) c")).then_inc(prev_in, 16)
                for c in range(KC // 2):
                    if c >= 2:
                        sp.wait_ge(proj_done, 6 * (c - 1))
                    s = E_XBC + 256 * c
                    sp.dma_start(w[:, c % 2, :, :], e.w_in_even[0, :, s:s + 256].rearrange("(k p) n -> p k n", p=P)).then_inc(w_in[c % 2], 16)
                    if c == 0:
                        sp.dma_start(wdt[:, :, :], e.w_in_even[0, :, E_DT:E_END].rearrange("(k p) n -> p k n", p=P)).then_inc(dt_in, 16)
                sp.dma_start(S.w_zb[:, :, :], e.w_in_even[0, :, E_ZB:E_XBC].rearrange("(k p) n -> p k n", p=P)).then_inc(S.w_zb_in, 16)
                sp.wait_ge(cv_copied, 3)
                sp.dma_start(e.outs[6][0, 0], cvrow[0:3, :]).then_inc(out, 16)
                sp.dma_start(e.outs[7][0].rearrange("b t c -> (b t) c"), cvrow[3:27, :]).then_inc(out, 16)
                sp.wait_ge(out, 32)

            @block.tensor
            def _(pe):
                pe.wait_ge(prev_in, 16)
                for f in range(KC):
                    last = nc.tensor.transpose(e.ps[:, 6, f * 24:(f + 1) * 24], prow[:, f * P:(f + 1) * P], e.ident[0:24, 0:24])
                last.then_inc(prev_done, 1)
                pe.wait_ge(dt_in, 16)
                for m in range(NT):
                    for k in range(KD):
                        last = mm(nc, e.ps[0:rows(m), 7, m * SH:(m + 1) * SH], hT[:, k, m * P:m * P + rows(m)], wdt[:, k, :], k == 0, k == KD - 1)
                last.then_inc(dt_done, 1)
                for f in range(KC):
                    if f % 2 == 0:
                        pe.wait_ge(w_in[f // 2 % 2], 16 * (f // 4 + 1))
                    for c, (s, n) in enumerate(CHUNKS):
                        g = 3 * f + c
                        if g >= 6:
                            pe.wait_ge(raw_ready, g - 5)
                        for k in range(KD):
                            last = mm(nc, e.ps[:, g % 6, 0:n], w[:, f // 2 % 2, k, (f % 2) * P:(f % 2 + 1) * P], hT[:, k, s:s + n], k == 0, k == KD - 1)
                        last.then_inc(proj_done, 1)
                pe.wait_ge(kept, KC)
                pe.wait_ge(raw_ready, NG)
                for f in range(KC):
                    last = nc.tensor.transpose(e.ps[0:27, f // 4, (f % 4) * P:(f % 4 + 1) * P], cv[:, f, :], e.ident)
                last.then_inc(cv_turned, 1)

            @block.scalar
            def _(act):
                act.wait_ge(dt_done, 1)
                act.wait_ge(abs_ready, 1)
                nc.scalar.activation(x2[:, :, :], x2[:, :, :], ACT.Exp, scale=-1.0).then_inc(dt_act, 1)
                act.wait_ge(abs_ready, 2)
                nc.scalar.activation(x1[:, :, :], x3[:, :, :], ACT.Ln)
                nc.scalar.activation(S.ea[:, :], e.ssd_row[:, 1, :], ACT.Exp).then_inc(dt_act, 1)
                act.wait_ge(zeroed, 1)

                def silu(f):
                    act.wait_ge(conv_done, f + 1)
                    nc.scalar.activation(S.convT[:, f, :], acc[:, f % 2, :], ACT.Silu).then_inc(act_done, 1)

                for f in range(KC):
                    if f >= 2:
                        act.wait_ge(conv_done, f - 1)
                        act.wait_ge(kept, f - 1)
                    for c, (s, n) in enumerate(CHUNKS):
                        g = 3 * f + c
                        act.wait_ge(proj_done, g + 1)
                        if c < 2:
                            nc.scalar.copy(raw[:, f % 2, 3 + s:3 + s + n], e.ps[:, g % 6, 0:n]).then_inc(raw_ready, 1)
                        else:
                            nc.scalar.copy(raw[:, f % 2, 3 + s:3 + TP], e.ps[:, g % 6, 0:LAST])
                            nc.scalar.copy(raws[:, f % 2, :, 3:3 + DS], e.ps[:, g % 6, LAST:n].rearrange("p (b t) -> p b t", t=DS)).then_inc(raw_ready, 1)
                    if f:
                        silu(f - 1)
                silu(KC - 1)
                for b in range(3):
                    act.wait_ge(cv_turned, 1)
                    nc.scalar.copy(cvrow[:, b * 512:(b + 1) * 512], e.ps[0:27, b, :]).then_inc(cv_copied, 1)

            @block.gpsimd
            def _(pool):
                nc.gpsimd.memset(S.xd[:, :, :], 0.0)
                nc.gpsimd.memset(raw[:, :, 0:3], 0.0).then_inc(zeroed, 1)
                for f in range(KC):
                    pool.wait_ge(raw_ready, 3 * (f + 1))
                    nc.gpsimd.tensor_copy(cv[:, f, 0:3], raw[:, f % 2, TP:TP + 3])
                    nc.gpsimd.tensor_copy(cv[:, f, 3:27].rearrange("p (b t) -> p b t", t=3), raws[:, f % 2, :, DS:DS + 3]).then_inc(kept, 1)

            @block.vector
            def _(dve):
                link = make_link(dve, e.dve_step, e.dve_n)
                dve.wait_ge(prev_done, 1)
                link(nc.vector.tensor_copy(prevT[:, :, :], e.ps[:, 6, 0:KC * 24].rearrange("p (f x) -> p f x", f=KC)))
                dve.wait_ge(dt_done, 1)
                dve.wait_ge(zeroed, 1)
                bias = e.ssd_row[:, 0, :]
                nc.vector.tensor_tensor(S.xd[:, 0:NTP, :], e.ps[:, 7, 0:NTP * SH].rearrange("p (m h) -> p m h", h=SH),
                                        bias[:, None, :].broadcast_to([P, NTP, SH]), ALU.add)
                link(nc.vector.tensor_tensor(S.xd[0:TS, NTP, :], e.ps[0:TS, 7, NTP * SH:NT * SH], bias[0:TS, :], ALU.add))
                link(nc.vector.tensor_scalar(x1[:, :, :], S.xd[:, :, :], -1.0, None, ALU.mult))
                nc.vector.tensor_tensor(x2[:, :, :], S.xd[:, :, :], x1[:, :, :], ALU.max).then_inc(abs_ready, 1)
                dve.wait_ge(dt_act, 1)
                nc.vector.tensor_scalar(x3[:, :, :], x2[:, :, :], 1.0, None, ALU.add).then_inc(abs_ready, 1)
                dve.wait_ge(dt_act, 2)
                x4 = acc[:, 0, 0:NT * SH].rearrange("p (m h) -> p m h", h=SH)
                link(nc.vector.tensor_scalar(x4, x3[:, :, :], 1.0, None, ALU.subtract))
                link(nc.vector.tensor_tensor(x2[:, :, :], x2[:, :, :], x4, ALU.subtract))
                link(nc.vector.reciprocal(x3[:, :, :], x3[:, :, :]))
                link(nc.vector.tensor_tensor(x2[:, :, :], x2[:, :, :], x3[:, :, :], ALU.mult))
                link(nc.vector.tensor_tensor(x2[:, :, :], x2[:, :, :], x1[:, :, :], ALU.add))
                link(nc.vector.scalar_tensor_tensor(S.xd[:, :, :], S.xd[:, :, :], 0.0, x2[:, :, :], ALU.max, ALU.add))
                link(nc.vector.scalar_tensor_tensor(S.dta[:, :, :], S.xd[:, :, :], -1.0, S.ea[:, None, :].broadcast_to([P, NT, SH]), ALU.mult, ALU.mult))
                for f in range(KC):
                    if f >= 2:
                        dve.wait_ge(raw_ready, 3 * (f - 1))
                    dve.wait_ge(raw_ready, 3 * f + 3)
                    link(nc.vector.tensor_copy(raws[:, f % 2, :, 0:3], prevT[:, f, :].rearrange("p (b t) -> p b t", t=3)))
                    if f >= 2:
                        dve.wait_ge(act_done, f - 1)
                    tap = lambda i: e.vec[:, NVEC + i * KC + f:NVEC + i * KC + f + 1]
                    b = e.vec[:, VEC["conv_b"][0] + f:VEC["conv_b"][0] + f + 1]
                    x, xs = acc[:, f % 2, 0:TP], acc[:, f % 2, TP:T].rearrange("p (b t) -> p b t", t=DS)
                    nc.vector.tensor_scalar(x, raw[:, f % 2, 0:TP], tap(0), b, ALU.mult, ALU.add)
                    link(nc.vector.tensor_scalar(xs, raws[:, f % 2, :, 0:DS], tap(0), b, ALU.mult, ALU.add))
                    for i in range(1, 4):
                        nc.vector.scalar_tensor_tensor(x, raw[:, f % 2, i:i + TP], tap(i), x, ALU.mult, ALU.add)
                        last = nc.vector.scalar_tensor_tensor(xs, raws[:, f % 2, :, i:i + DS], tap(i), xs, ALU.mult, ALU.add)
                        if i < 3:
                            link(last)
                    last.then_inc(conv_done, 1)
    end_block(nc)


def block_ssd_scan(nc, e, hT, S):
    UNITS = ("cb", "xs", "cum0", "cum1", "z", "inter", "yT", "intra", "upd")
    TAKERS = {"cb": ("dve", "act"), "xs": ("act",), "cum0": ("dve",), "cum1": ("dve",), "z": ("act",), "inter": ("dve",),
              "yT": ("dve",), "intra": ("dve",), "upd": ("dve",)}
    with ExitStack() as ctx:
        def sb(name, shape, dt=F32):
            return ctx.enter_context(nc.sbuf_tensor(name, shape, dt))
        w = S.w_zb
        cc, bt = sb("cb_cum", [P, 2, 288]), sb("b_rows", [P, 2, 256])
        sm = sb("decays", [P, 2, 3, SH])
        ones = e.F["tri"][:, P - 1:P].broadcast_to([P, P])
        xsb, xdt, xdt2, y, zs = (sb(s, [P, 2, SI]) for s in ("xs_rows", "x_dt", "x_dt_decayed", "y_rows", "silu_z_b"))
        L = sb("decay_matrix", [P, 2, 2, 8, P])
        h, hdec = S.h, sb("h_decayed", [P, SI])
        ss = sb("y_norm", [P, 2, 1])
        out = e.stored["ssd_state"]
        done = {u: new_sem(nc, f"scan_{u}_done") for u in UNITS}
        taken = {(u, t): new_sem(nc, f"scan_{u}_taken_{t}") for u in UNITS for t in TAKERS[u]}
        names = ("small_ready", "decays_ready", "L_ready", "W_ready", "xdt_ready", "xdt2_ready", "hdec_ready", "y_summed", "y_gated", "y_squared", "var_ready", "std_ready", "yn_ready", "h_ready")
        small, decays, L_ready, W_ready, xdt_ready, xdt2_ready, hdec_ready, y_summed, y_gated, y_squared, var_ready, std_ready, yn_ready, h_ready = \
            (new_sem(nc, "scan_" + s) for s in names)
        order = [(u, i if u != "yT" else i - 1) for i in range(NTP) for u in UNITS if not (u == "yT" and i == 0)] + [("yT", NTP - 1), ("out", 0)]
        pair = {ui: 2 * (n % 4) for n, ui in enumerate(order)}
        before = {ui: order[n - 4] for n, ui in enumerate(order) if n >= 4}

        with nc.Block() as block:
            @block.sync
            def _(sp):
                sp.wait_ge(std_ready, NTP + 1)
                sp.dma_start(e.outs[8][0, 0].rearrange("(j q) p n -> (q p) j n", q=2), zs[:, 0, :].rearrange("p (j n) -> p j n", n=SN)).then_inc(out, 16)
                sp.wait_ge(out, 16)

            @block.tensor
            def _(pe):
                def unit(u, i):
                    if (u, i) in before:
                        b = before[(u, i)]
                        for t in TAKERS[b[0]]:
                            pe.wait_ge(taken[b[0], t], b[1] + 1)
                    return pair[(u, i)]

                for u, i in order:
                    b = unit(u, i)
                    tok = slice(i * P, (i + 1) * P)
                    if u == "cb":
                        for g in range(G):
                            mm(nc, e.ps[:, b, g * P:(g + 1) * P], S.convT[:, 8 + g, tok], S.convT[:, 10 + g, tok], True, True)
                        mm(nc, e.ps[:, b, 256:256 + SH], e.F["tri"], S.dta[:, i, :], True, True)
                        mm(nc, e.ps[:, b, 272:272 + SH], ones, S.dta[:, i, :], True, True)
                        for g in range(G):
                            last = nc.tensor.transpose(e.ps[:, b + 1, g * P:(g + 1) * P], S.convT[:, 8 + g, tok], e.ident)
                    elif u == "xs":
                        for j in range(8):
                            last = nc.tensor.transpose(e.ps[:, b + j // 4, (j % 4) * P:(j % 4 + 1) * P], S.convT[:, j, tok], e.ident)
                    elif u in ("cum0", "cum1"):
                        for hh in range(8):
                            hd = 8 * int(u[3]) + hh
                            mm(nc, e.ps[:, b + hh // 4, (hh % 4) * P:(hh % 4 + 1) * P], S.dta[:, i, hd:hd + 1].broadcast_to([P, P]), e.F["tri"], hh % 4 == 0, False)
                            if hh % 4 == 3:
                                last = mm(nc, e.ps[:, b + hh // 4, :].rearrange("p (h t) -> p h t", h=4), e.identb, e.B["later"][:, None, :].broadcast_to([P, 4, P]), False, True)
                    elif u == "z":
                        if i == 0:
                            pe.wait_ge(S.w_zb_in, 16)
                        for c in range(2):
                            for k in range(KD):
                                last = mm(nc, e.ps[:, b + c, :], hT[:, k, tok], w[:, k, 512 * c:512 * (c + 1)], k == 0, k == KD - 1)
                    elif u == "inter":
                        pe.wait_ge(h_ready, i + 1)
                        for g in range(G):
                            last = mm(nc, e.ps[:, b + g, :], S.convT[:, 10 + g, tok], h[:, g * 512:(g + 1) * 512], True, True)
                    elif u == "intra":
                        pe.wait_ge(xdt_ready, i + 1)
                        for hd in range(SH):
                            if hd % 8 == 0:
                                pe.wait_ge(W_ready, 2 * i + hd // 8 + 1)
                            last = mm(nc, e.ps[:, b + hd // 8, (hd % 8) * SP_:(hd % 8 + 1) * SP_], L[:, i % 2, hd // 8, hd % 8, :],
                                      xdt[:, i % 2, hd * SP_:(hd + 1) * SP_], True, True)
                    elif u == "upd":
                        pe.wait_ge(xdt2_ready, i + 1)
                        pe.wait_ge(taken["cb", "act"], i + 1)
                        for g in range(G):
                            last = mm(nc, e.ps[:, b + g, :], bt[:, i % 2, g * P:(g + 1) * P], xdt2[:, i % 2, g * 512:(g + 1) * 512], True, True)
                    elif u == "yT":
                        pe.wait_ge(yn_ready, i + 1)
                        for j in range(8):
                            last = nc.tensor.transpose(e.ps[:, b + j // 4, (j % 4) * P:(j % 4 + 1) * P], y[:, i % 2, j * P:(j + 1) * P], e.ident)
                    else:
                        pe.wait_ge(h_ready, NTP + 1)
                        for j in range(8):
                            last = nc.tensor.transpose(e.ps[:, b + j // 4, (j % 4) * P:(j % 4 + 1) * P], h[:, j * P:(j + 1) * P], e.ident)
                        last.then_inc(done["z"], 1)
                        continue
                    last.then_inc(done[u], 1)

            def both(u, i):
                b = pair[(u, i)]
                return e.ps[:, b:b + 2, :]

            @block.scalar
            def _(act):
                link = make_link(act, e.act_step, e.act_n)

                def norm(i):
                    act.wait_ge(y_gated, i + 1)
                    nc.scalar.activation(zs[:, i % 2, :], y[:, i % 2, :], ACT.Square, accum_out=ss[:, i % 2, :]).then_inc(y_squared, 1)
                    act.wait_ge(var_ready, i + 1)
                    nc.scalar.activation(ss[:, i % 2, :], ss[:, i % 2, :], ACT.Sqrt).then_inc(std_ready, 1)
                    act.wait_ge(std_ready, i + 1)
                    nc.scalar.activation(y[:, i % 2, :], y[:, i % 2, :], ACT.Copy, scale=ss[:, i % 2, :]).then_inc(yn_ready, 1)

                for i in range(NTP):
                    act.wait_ge(done["cb"], i + 1)
                    if i >= 2:
                        act.wait_ge(done["upd"], i - 1)
                    nc.scalar.copy(bt[:, i % 2, :], e.ps[:, pair[("cb", i)] + 1, 0:256]).then_inc(taken["cb", "act"], 1)
                    act.wait_ge(small, i + 1)
                    nc.scalar.activation(sm[:, i % 2, :, :], sm[:, i % 2, :, :], ACT.Exp).then_inc(decays, 1)
                    act.wait_ge(done["xs"], i + 1)
                    if i >= 2:
                        act.wait_ge(y_gated, i - 1)
                    nc.scalar.copy(xsb[:, i % 2, :].rearrange("p (b n) -> p b n", b=2), both("xs", i)).then_inc(taken["xs", "act"], 1)
                    for c in range(2):
                        act.wait_ge(taken[f"cum{c}", "dve"], i + 1)
                        nc.scalar.activation(L[:, i % 2, c, :, :], L[:, i % 2, c, :, :], ACT.Exp).then_inc(L_ready, 1)
                    if i:
                        norm(i - 1)
                    act.wait_ge(done["z"], i + 1)
                    nc.scalar.activation(zs[:, i % 2, :].rearrange("p (b n) -> p b n", b=2), both("z", i), ACT.Silu).then_inc(taken["z", "act"], 1)
                norm(NTP - 1)
                act.wait_ge(done["z"], NTP + 1)
                nc.scalar.copy(zs[:, 0, :].rearrange("p (b n) -> p b n", b=2), both("out", 0)).then_inc(std_ready, 1)

            @block.gpsimd
            def _(pool):
                link = make_link(pool, e.pool_step, e.pool_n)
                nc.gpsimd.memset(h[:, :], 0.0).then_inc(h_ready, 1)
                for i in range(NTP):
                    v = lambda t: t[:, i % 2, :].rearrange("p (h q) -> p h q", h=SH)
                    bc = lambda t: t[:, :, None].broadcast_to([P, SH, SP_])
                    pool.wait_ge(taken["xs", "act"], i + 1)
                    if i >= 2:
                        pool.wait_ge(done["upd"], i - 1)
                    link(nc.gpsimd.tensor_tensor(v(xdt), v(xsb), bc(S.xd[:, i, :]), ALU.mult))
                    pool.sem_inc(xdt_ready, 1)
                    pool.wait_ge(decays, i + 1)
                    nc.gpsimd.tensor_tensor(v(xdt2), v(xdt), bc(sm[:, i % 2, 1, :]), ALU.mult).then_inc(xdt2_ready, 1)
                    pool.wait_ge(h_ready, i + 1)
                    if i:
                        pool.wait_ge(taken["upd", "dve"], i)
                    nc.gpsimd.tensor_tensor(hdec[:, :].rearrange("p (h q) -> p h q", h=SH), h[:, :].rearrange("p (h q) -> p h q", h=SH),
                                            bc(sm[:, i % 2, 2, :]), ALU.mult).then_inc(hdec_ready, 1)
                    link(nc.gpsimd.tensor_tensor(v(xsb), v(xsb), bc(e.ssd_row[:, 2, :]), ALU.mult))
                    pool.wait_ge(taken["intra", "dve"], i + 1)
                    link(nc.gpsimd.tensor_tensor(y[:, i % 2, :], y[:, i % 2, :], xsb[:, i % 2, :], ALU.add))
                    pool.wait_ge(taken["z", "act"], i + 1)
                    nc.gpsimd.tensor_tensor(y[:, i % 2, :], y[:, i % 2, :], zs[:, i % 2, :], ALU.mult).then_inc(y_gated, 1)

            @block.vector
            def _(dve):
                link = make_link(dve, e.dve_step, e.dve_n)

                def put_yT(i):
                    dve.wait_ge(done["yT"], i + 1)
                    s = VEC["ssd_norm"][0]
                    nc.vector.tensor_tensor(S.convT[:, 0:8, i * P:(i + 1) * P], both("yT", i).rearrange("p b (j t) -> p (b j) t", j=4),
                                            e.vec[:, s:s + 8][:, :, None].broadcast_to([P, 8, P]), ALU.mult).then_inc(taken["yT", "dve"], 1)

                def variance(i):
                    dve.wait_ge(y_squared, i + 1)
                    link(nc.vector.tensor_scalar(ss[:, i % 2, :], ss[:, i % 2, :], 1.0 / SI, EPS, ALU.mult, ALU.add))
                    nc.vector.reciprocal(ss[:, i % 2, :], ss[:, i % 2, :]).then_inc(var_ready, 1)

                for i in range(NTP):
                    k = i % 2
                    dve.wait_ge(done["cb"], i + 1)
                    nc.vector.tensor_copy(cc[:, k, :], e.ps[:, pair[("cb", i)], 0:288]).then_inc(taken["cb", "dve"], 1)
                    dve.wait_ge(taken["cb", "dve"], i + 1)
                    nc.vector.tensor_copy(sm[:, k, 0, :], cc[:, k, 256:272])
                    nc.vector.tensor_copy(sm[:, k, 2, :], cc[:, k, 272:288])
                    nc.vector.tensor_tensor(sm[:, k, 1, :], cc[:, k, 272:288], cc[:, k, 256:272], ALU.subtract).then_inc(small, 1)
                    for c in range(2):
                        dve.wait_ge(done[f"cum{c}"], i + 1)
                        nc.vector.tensor_tensor(L[:, k, c, :, :], both(f"cum{c}", i).rearrange("p b (h t) -> p (b h) t", h=4),
                                                cc[:, k, 256 + 8 * c:264 + 8 * c][:, :, None].broadcast_to([P, 8, P]), ALU.subtract).then_inc(taken[f"cum{c}", "dve"], 1)
                    for c in range(2):
                        dve.wait_ge(L_ready, 2 * i + c + 1)
                        nc.vector.tensor_tensor(L[:, k, c, :, :], L[:, k, c, :, :], cc[:, k, c * P:(c + 1) * P][:, None, :].broadcast_to([P, 8, P]), ALU.mult).then_inc(W_ready, 1)
                    if i:
                        variance(i - 1)
                    dve.wait_ge(done["inter"], i + 1)
                    dve.wait_ge(decays, i + 1)
                    nc.vector.tensor_tensor(y[:, k, :].rearrange("p (h q) -> p h q", h=SH), both("inter", i).rearrange("p b (h q) -> p (b h) q", h=8),
                                            sm[:, k, 0, :][:, :, None].broadcast_to([P, SH, SP_]), ALU.mult).then_inc(taken["inter", "dve"], 1)
                    if i:
                        put_yT(i - 1)
                    dve.wait_ge(done["intra"], i + 1)
                    dve.wait_ge(taken["inter", "dve"], i + 1)
                    yv = y[:, k, :].rearrange("p (b n) -> p b n", b=2)
                    nc.vector.tensor_tensor(yv, both("intra", i), yv, ALU.add).then_inc(taken["intra", "dve"], 1)
                    dve.wait_ge(done["upd"], i + 1)
                    dve.wait_ge(hdec_ready, i + 1)
                    nc.vector.tensor_tensor(h[:, :].rearrange("p (b n) -> p b n", b=2), both("upd", i), hdec[:, :].rearrange("p (b n) -> p b n", b=2),
                                            ALU.add).then_inc(taken["upd", "dve"], 1)
                    dve.wait_ge(taken["upd", "dve"], i + 1)
                    dve.sem_inc(h_ready, 1)
                variance(NTP - 1)
                put_yT(NTP - 1)
    end_block(nc)




def block_ssd_samples(nc, e, hT, S):
    R = TS
    tok = slice(TP, T)
    with ExitStack() as ctx:
        def sb(name, shape, dt=F32):
            return ctx.enter_context(nc.sbuf_tensor(name, shape, dt))
        cc, sm, bt = sb("cb_cum_s", [R, 96]), sb("decays_s", [R, 2, SH]), sb("b_rows_s", [R, G, P])
        CTm, Bm = sb("c_T_masked", [P, G, DB, R]), sb("b_rows_masked", [R, G, DB, P])
        ecs = sb("state_decay", [P, 8, DB])
        xsb, xdt, xdt2, y, zs, L = (sb(s + "_s", [R, n]) for s, n in (("xs_rows", SI), ("x_dt", SI), ("x_dt_decayed", SI), ("y_rows", SI), ("silu_z_b", SI), ("decay_matrix", SH * R)))
        tmp, ss = sb("y_tmp_s", [R, SI]), sb("y_norm_s", [R, 1])
        nat, nd, hbT = sb("state_in", [P, 2, 8, SN]), sb("state_new", [P, 2, 8, SN]), sb("state_T", [P, 2, SI])
        sem = lambda s: new_sem(nc, "ssds_" + s)
        nat_in, st_out = [sem("state_in0"), sem("state_in1")], [e.stored["ssd_states0"], e.stored["ssd_states1"]]
        s1_done, xs_done, z_done, bank6_free, bank7_free, xs_taken, z_taken = (sem(s) for s in ("stage1", "xs", "z", "bank6_free", "bank7_free", "xs_taken", "z_taken"))
        dta_wide, exps_in, exps_out, L_ready, xdt_ready, prep_ready = (sem(s) for s in ("dta_wide", "exps_in", "exps_out", "L_ready", "xdt_ready", "masked_ready"))
        st_turned, hb_ready, inter_done, upd_done, nd_ready, upd_taken, W_ready, intra_done = (sem(s) for s in ("state_turned", "state_T_ready", "inter", "upd", "decayed", "upd_taken", "W_ready", "intra"))
        y_summed, y_gated, sq_done, var_ready, yn_ready, yT_done = (sem(s) for s in ("y_summed", "y_gated", "squared", "var_ready", "yn_ready", "yT"))
        with nc.Block() as block:
            @block.sync
            def _(sp):
                for b in range(DB):
                    if b >= 2:
                        sp.wait_ge(upd_taken, b - 1)
                    sp.dma_start(nat[:, b % 2, :, :], e.state_ssd[0, b].rearrange("(j q) p n -> (q p) j n", q=2)).then_inc(nat_in[b % 2], 16)

            @block.gpsimd
            def _(pool):
                link = make_link(pool, e.pool_step, e.pool_n)
                nc.gpsimd.tensor_copy(tmp[:, :].rearrange("p (h q) -> p h q", h=SH), S.dta[0:R, NTP, :][:, :, None].broadcast_to([R, SH, SP_])).then_inc(dta_wide, 1)
                for g in range(G):
                    nc.gpsimd.tensor_tensor(CTm[:, g, :, :], S.convT[:, 10 + g, tok][:, None, :].broadcast_to([P, DB, R]),
                                            e.F["bmask"].rearrange("p (b t) -> p b t", b=DB), ALU.mult)
                pool.wait_ge(bank6_free, 1)
                for g in range(G):
                    last = nc.gpsimd.tensor_tensor(Bm[:, g, :, :], bt[:, g, :][:, None, :].broadcast_to([R, DB, P]),
                                                   e.F["bcol"][0:R, :][:, :, None].broadcast_to([R, DB, P]), ALU.mult)
                last.then_inc(prep_ready, 1)
                v = lambda t: t[:, :].rearrange("p (h q) -> p h q", h=SH)
                bc = lambda t: t[:, :, None].broadcast_to([R, SH, SP_])
                pool.wait_ge(xs_taken, 1)
                link(nc.gpsimd.tensor_tensor(v(xdt), v(xsb), bc(S.xd[0:R, NTP, :]), ALU.mult))
                link(nc.gpsimd.tensor_tensor(v(xsb), v(xsb), bc(e.ssd_row[0:R, 2, :]), ALU.mult))
                pool.wait_ge(exps_out, 2)
                nc.gpsimd.tensor_tensor(v(xdt2), v(xdt), bc(sm[:, 1, :]), ALU.mult).then_inc(xdt_ready, 1)
                for b in range(DB):
                    pool.wait_ge(nat_in[b % 2], 16 * (b // 2 + 1))
                    if b >= 2:
                        pool.wait_ge(st_out[b % 2], 16 * (b // 2))
                    nc.gpsimd.tensor_tensor(nd[:, b % 2, :, :], nat[:, b % 2, :, :], ecs[:, :, b][:, :, None].broadcast_to([P, 8, SN]), ALU.mult).then_inc(nd_ready, 1)
                pool.wait_ge(y_summed, 1)
                pool.wait_ge(z_taken, 1)
                link(nc.gpsimd.tensor_tensor(y[:, :], y[:, :], xsb[:, :], ALU.add))
                nc.gpsimd.tensor_tensor(y[:, :], y[:, :], zs[:, :], ALU.mult).then_inc(y_gated, 1)

            @block.tensor
            def _(pe):
                for g in range(G):
                    mm(nc, e.ps[0:R, 6, g * R:(g + 1) * R], S.convT[:, 8 + g, tok], S.convT[:, 10 + g, tok], True, True)
                    nc.tensor.transpose(e.ps[0:R, 6, 96 + g * P:96 + (g + 1) * P], S.convT[:, 8 + g, tok], e.ident)
                mm(nc, e.ps[0:R, 6, 64:80], e.F["trib"][0:R, :], S.dta[0:R, NTP, :], True, True)
                mm(nc, e.ps[0:R, 6, 80:96], e.F["oneb"][0:R, :], S.dta[0:R, NTP, :], True, True)
                pe.wait_ge(dta_wide, 1)
                for j in range(8):
                    mm(nc, e.ps[:, 6, 384 + 8 * j:392 + 8 * j], tmp[:, j * P:(j + 1) * P], e.F["bcol"][0:R, :], True, True)
                for hd in range(SH):
                    mm(nc, e.ps[0:R, 7, hd * R:(hd + 1) * R], S.dta[0:R, NTP, hd:hd + 1].broadcast_to([R, R]), e.F["trib"][0:R, :], hd == 0, False)
                mm(nc, e.ps[0:R, 7, :].rearrange("p (h t) -> p h t", h=SH), e.identb[0:R, 0:R], e.B["laterb"][0:R, :][:, None, :].broadcast_to([R, SH, R]),
                   False, True).then_inc(s1_done, 1)
                for j in range(8):
                    last = nc.tensor.transpose(e.ps[0:R, j // 4, (j % 4) * P:(j % 4 + 1) * P], S.convT[:, j, tok], e.ident)
                last.then_inc(xs_done, 1)
                for c in range(2):
                    for k in range(KD):
                        last = mm(nc, e.ps[0:R, 2 + c, :], hT[:, k, tok], S.w_zb[:, k, 512 * c:512 * (c + 1)], k == 0, k == KD - 1)
                last.then_inc(z_done, 1)
                pe.wait_ge(prep_ready, 1)
                pe.wait_ge(xdt_ready, 1)
                pe.wait_ge(bank6_free, 2)
                pe.wait_ge(bank7_free, 1)
                for b in range(DB):
                    pe.wait_ge(nat_in[b % 2], 16 * (b // 2 + 1))
                    if b < 2:
                        pe.wait_ge((xs_taken, z_taken)[b], 1)
                    else:
                        pe.wait_ge(hb_ready, b - 1)
                    for j in range(8):
                        last = nc.tensor.transpose(e.ps[:, 2 * (b % 2) + j // 4, (j % 4) * P:(j % 4 + 1) * P], nat[:, b % 2, j, :], e.ident)
                    last.then_inc(st_turned, 1)
                    if b:
                        pe.wait_ge(upd_taken, b)
                    for j in range(8):
                        last = mm(nc, e.ps[:, 6 + j // 4, (j % 4) * P:(j % 4 + 1) * P], xdt2[:, j * P:(j + 1) * P], Bm[:, j // 4, b, :], True, True)
                    last.then_inc(upd_done, 1)
                    pe.wait_ge(hb_ready, b + 1)
                    for g in range(G):
                        last = mm(nc, e.ps[0:R, 4 + g, :], CTm[:, g, b, :], hbT[:, b % 2, g * 512:(g + 1) * 512], b == 0, b == DB - 1)
                    last.then_inc(inter_done, 1)
                pe.wait_ge(W_ready, 1)
                for hd in range(SH):
                    last = mm(nc, e.ps[0:R, hd // 8, (hd % 8) * SP_:(hd % 8 + 1) * SP_], L[:, hd * R:(hd + 1) * R], xdt[:, hd * SP_:(hd + 1) * SP_], True, True)
                last.then_inc(intra_done, 1)
                pe.wait_ge(yn_ready, 1)
                for j in range(8):
                    last = nc.tensor.transpose(e.ps[:, 2, j * R:(j + 1) * R], y[:, j * P:(j + 1) * P], e.ident[0:R, 0:R])
                last.then_inc(yT_done, 1)

            def store(act, b):
                act.wait_ge(upd_taken, b + 1)
                act.dma_start(e.outs[9][0, b].rearrange("(j q) p n -> (q p) j n", q=2), nd[:, b % 2, :, :]).then_inc(st_out[b % 2], 16)

            @block.scalar
            def _(act):
                act.wait_ge(exps_in, 1)
                nc.scalar.activation(ecs[:, :, :], ecs[:, :, :], ACT.Exp).then_inc(exps_out, 1)
                nc.scalar.activation(sm[:, :, :], sm[:, :, :], ACT.Exp).then_inc(exps_out, 1)
                act.wait_ge(xs_done, 1)
                nc.scalar.copy(xsb[:, :].rearrange("p (b n) -> p b n", b=2), e.ps[0:R, 0:2, :]).then_inc(xs_taken, 1)
                act.wait_ge(L_ready, 1)
                nc.scalar.activation(L[:, :], L[:, :], ACT.Exp).then_inc(L_ready, 1)
                act.wait_ge(z_done, 1)
                nc.scalar.activation(zs[:, :].rearrange("p (b n) -> p b n", b=2), e.ps[0:R, 2:4, :], ACT.Silu).then_inc(z_taken, 1)
                for b in range(DB):
                    act.wait_ge(st_turned, b + 1)
                    if b >= 2:
                        act.wait_ge(inter_done, b - 1)
                    nc.scalar.copy(hbT[:, b % 2, :].rearrange("p (b n) -> p b n", b=2), e.ps[:, 2 * (b % 2):2 * (b % 2) + 2, :]).then_inc(hb_ready, 1)
                    if b:
                        store(act, b - 1)
                store(act, DB - 1)
                act.wait_ge(y_gated, 1)
                nc.scalar.activation(tmp[:, :], y[:, :], ACT.Square, accum_out=ss[:, :]).then_inc(sq_done, 1)
                act.wait_ge(var_ready, 1)
                nc.scalar.activation(ss[:, :], ss[:, :], ACT.Sqrt).then_inc(sq_done, 1)
                act.wait_ge(sq_done, 2)
                nc.scalar.activation(y[:, :], y[:, :], ACT.Copy, scale=ss[:, :]).then_inc(yn_ready, 1)
                for b in range(2):
                    act.wait_ge(st_out[b], 16 * DB // 2)

            @block.vector
            def _(dve):
                link = make_link(dve, e.dve_step, e.dve_n)
                dve.wait_ge(s1_done, 1)
                link(nc.vector.tensor_copy(cc[:, :], e.ps[0:R, 6, 0:96]))
                nc.vector.tensor_copy(bt[:, :, :], e.ps[0:R, 6, 96:352].rearrange("p (g n) -> p g n", g=G)).then_inc(bank6_free, 1)
                nc.vector.tensor_copy(sm[:, 0, :], cc[:, 64:80])
                nc.vector.tensor_tensor(sm[:, 1, :], cc[:, 80:96], cc[:, 64:80], ALU.subtract)
                link(nc.vector.tensor_copy(ecs[:, :, :], e.ps[:, 6, 384:448].rearrange("p (j b) -> p j b", j=8)))
                dve.sem_inc(exps_in, 1)
                dve.sem_inc(bank6_free, 1)
                link(nc.vector.tensor_tensor(L[:, :].rearrange("p (h t) -> p h t", h=SH), e.ps[0:R, 7, :].rearrange("p (h t) -> p h t", h=SH),
                                             cc[:, 64:80][:, :, None].broadcast_to([R, SH, R]), ALU.subtract))
                dve.sem_inc(bank7_free, 1)
                dve.sem_inc(L_ready, 1)
                dve.wait_ge(L_ready, 2)
                for g in range(G):
                    Lv = L[:, g * 256:(g + 1) * 256].rearrange("p (h t) -> p h t", h=8)
                    last = nc.vector.tensor_tensor(Lv, Lv, cc[:, g * R:(g + 1) * R][:, None, :].broadcast_to([R, 8, R]), ALU.mult)
                last.then_inc(W_ready, 1)
                for b in range(DB):
                    dve.wait_ge(upd_done, b + 1)
                    dve.wait_ge(nd_ready, b + 1)
                    v = nd[:, b % 2, :, :].rearrange("p (c j) n -> p c (j n)", c=2)
                    nc.vector.tensor_tensor(v, e.ps[:, 6:8, :], v, ALU.add).then_inc(upd_taken, 1)
                dve.wait_ge(inter_done, DB)
                yv = y[:, :].rearrange("p (b n) -> p b n", b=2)
                link(nc.vector.tensor_tensor(y[:, :].rearrange("p (h q) -> p h q", h=SH), e.ps[0:R, 4:6, :].rearrange("p b (h q) -> p (b h) q", h=8),
                                             sm[:, 0, :][:, :, None].broadcast_to([R, SH, SP_]), ALU.mult))
                dve.wait_ge(intra_done, 1)
                nc.vector.tensor_tensor(yv, e.ps[0:R, 0:2, :], yv, ALU.add).then_inc(y_summed, 1)
                dve.wait_ge(sq_done, 1)
                link(nc.vector.tensor_scalar(ss[:, :], ss[:, :], 1.0 / SI, EPS, ALU.mult, ALU.add))
                nc.vector.reciprocal(ss[:, :], ss[:, :]).then_inc(var_ready, 1)
                dve.wait_ge(yT_done, 1)
                s = VEC["ssd_norm"][0]
                link(nc.vector.tensor_tensor(S.convT[:, 0:8, tok], e.ps[:, 2, 0:256].rearrange("p (j t) -> p j t", j=8),
                                             e.vec[:, s:s + 8][:, :, None].broadcast_to([P, 8, R]), ALU.mult))
    end_block(nc)


def block_out(nc, e, name, W, mix, pairs, l, xT, mods=()):
    K, KS, NB = 2 * len(mix), 2 * pairs, 6 if mods else 8
    with ExitStack() as ctx:
        def sb(suffix, shape, dt=F32):
            return ctx.enter_context(nc.sbuf_tensor(f"{name}_{suffix}", shape, dt))
        w, whi, wlo = sb("w", [P, 2, K, P]), sb("w_high", [P, 2, KS, P], F32R), sb("w_rest", [P, 2, KS, P], F32R)
        mhi, mlo = sb("mix_high", [P, KS, T], F32R), sb("mix_rest", [P, KS, T], F32R)
        tmp = sb("tmp", [P, 2, TS])
        wm = sb("w_mod", [P, KD, 512]) if mods else None
        mrow = sb("mod_rows", [9, D]) if mods else None
        sem = lambda s: new_sem(nc, f"{name}_{s}")
        mod_rows, mod_turned, mod_in, mod_done, mod_taken = sem("mod_rows_ready"), sem("mod_turned"), sem("w_mod_in"), sem("mod_done"), sem("mod_taken")
        w_in, x_in, done, taken = [sem("w_in0"), sem("w_in1")], sem("x_in"), sem("done"), sem("taken")
        w_high, w_rest, mix_high, mix_rest_dve, mix_rest_pool = (sem(s) for s in ("w_high_ready", "w_rest_ready", "mix_high_ready", "mix_rest_dve", "mix_rest_pool"))
        with nc.Block() as block:
            @block.sync
            def _(sp):
                for f in range(KD):
                    if f >= 2:
                        sp.wait_ge(done, 3 * (f - 1))
                    sp.dma_start(w[:, f % 2, :, :], W[:, f * P:(f + 1) * P].rearrange("(k p) n -> p k n", p=P)).then_inc(w_in[f % 2], 16)
                    if f == 1:
                        sp.dma_start(xT[:, :, :], e.x_save).then_inc(x_in, 16)

            @block.tensor
            def _(pe):
                for f in range(KD):
                    pe.wait_ge(w_in[f % 2], 16 * (f // 2 + 1))
                    for c, (s, n) in enumerate(CHUNKS):
                        g = 3 * f + c
                        if g >= NB:
                            pe.wait_ge(taken, g - NB + 1)
                        out = e.ps[:, g % NB, 0:n]
                        for k in range(KS, K):
                            mm(nc, out, w[:, f % 2, k, :], mix[k // 2][:, k % 2, s:s + n], k == KS, False)
                        if c == 0:
                            pe.wait_ge(w_rest, f + 1)
                        for k in range(KS):
                            if f == 0 and k % 2 == 0:
                                pe.wait_ge(*((mix_rest_dve, -(-pairs // 2) * c + k // 4 + 1) if k % 4 == 0 else (mix_rest_pool, pairs // 2 * c + k // 4 + 1)))
                            mm(nc, out, whi[:, f % 2, k, :], mhi[:, k, s:s + n], KS == K and k == 0, False)
                            mm(nc, out, whi[:, f % 2, k, :], mlo[:, k, s:s + n], False, False)
                            last = mm(nc, out, wlo[:, f % 2, k, :], mhi[:, k, s:s + n], False, k == KS - 1)
                        last.then_inc(done, 1)
                    if f < 2 * len(mods):
                        pe.wait_ge(mod_in, 16 * (f + 1))
                        if f >= 2 and f % 2 == 0:
                            pe.wait_ge(mod_taken, f // 2)
                        mod_products(nc, e, wm, 6 + f % 2).then_inc(mod_done, 1)
                        if f % 2 == 1:
                            pe.wait_ge(mod_rows, f // 2 + 1)
                            mod_turn(nc, e, mrow, 6, 0).then_inc(mod_turned, 1)

            @block.scalar
            def _(act):
                for j in range(2 * len(mods)):
                    if j:
                        act.wait_ge(mod_done, j)
                    load_mod_half(act, e, mods[j // 2][0], mods[j // 2][1], j % 2, wm[:, :, :], mod_in)
                    if j % 2 == 1:
                        act.wait_ge(mod_done, j + 1)
                        if j > 1:
                            act.wait_ge(mod_turned, j // 2)
                        nc.scalar.copy(mrow[:, :].rearrange("p (b n) -> p b n", b=2), e.ps[0:9, 6:8, :]).then_inc(mod_rows, 1)

            @block.gpsimd
            def _(pool):
                def w_part(f):
                    pool.wait_ge(w_high, f + 1)
                    nc.gpsimd.tensor_tensor(wlo[:, f % 2, :, :], w[:, f % 2, 0:KS, :], whi[:, f % 2, :, :].bitcast(F32), ALU.subtract).then_inc(w_rest, 1)

                w_part(0)
                for c, (s, n) in enumerate(CHUNKS):
                    for j in range(1, pairs, 2):
                        pool.wait_ge(mix_high, pairs * c + j + 1)
                        nc.gpsimd.tensor_tensor(mlo[:, 2 * j:2 * j + 2, s:s + n], mix[j][:, :, s:s + n], mhi[:, 2 * j:2 * j + 2, s:s + n].bitcast(F32), ALU.subtract).then_inc(mix_rest_pool, 1)
                for f in range(1, KD):
                    w_part(f)

            @block.vector
            def _(dve):
                link = make_link(dve, e.dve_step, e.dve_n)

                def finish(i):
                    dve.wait_ge(mod_turned, i + 1)
                    mod_finish(nc, e, link, mods[i][0], mods[i][1], 6, 0)
                    dve.sem_inc(mod_taken, 1)

                def w_part(f):
                    dve.wait_ge(w_in[f % 2], 16 * (f // 2 + 1))
                    nc.vector.tensor_copy(whi[:, f % 2, :, :], w[:, f % 2, 0:KS, :]).then_inc(w_high, 1)

                w_part(0)
                for c, (s, n) in enumerate(CHUNKS):
                    for j in range(pairs):
                        nc.vector.tensor_copy(mhi[:, 2 * j:2 * j + 2, s:s + n], mix[j][:, :, s:s + n]).then_inc(mix_high, 1)
                    for j in range(0, pairs, 2):
                        dve.wait_ge(mix_high, pairs * c + j + 1)
                        nc.vector.tensor_tensor(mlo[:, 2 * j:2 * j + 2, s:s + n], mix[j][:, :, s:s + n], mhi[:, 2 * j:2 * j + 2, s:s + n].bitcast(F32), ALU.subtract).then_inc(mix_rest_dve, 1)
                w_part(1)
                dve.wait_ge(x_in, 16)
                if mods:
                    finish(0)
                for f in range(KD):
                    for c, (s, n) in enumerate(CHUNKS):
                        g = 3 * f + c
                        dve.wait_ge(done, g + 1)
                        x = xT[:, f, s:s + n]
                        if c < 2:
                            nc.vector.scalar_tensor_tensor(x, e.ps[:, g % NB, 0:n], e.mod[:, l, 16 + f, 0:1], x, ALU.mult, ALU.add).then_inc(taken, 1)
                        else:
                            nc.vector.scalar_tensor_tensor(x[:, 0:LAST], e.ps[:, g % NB, 0:LAST], e.mod[:, l, 16 + f, 0:1], x[:, 0:LAST], ALU.mult, ALU.add)
                            link(nc.vector.tensor_tensor(tmp[:, f % 2, :].rearrange("p (b t) -> p b t", t=DS), e.ps[:, g % NB, LAST:n].rearrange("p (b t) -> p b t", t=DS),
                                                         e.mod[:, l, 16 + f, 1:9][:, :, None].broadcast_to([P, DB, DS]), ALU.mult))
                            nc.vector.tensor_tensor(x[:, LAST:n], x[:, LAST:n], tmp[:, f % 2, :], ALU.add).then_inc(taken, 1)
                            dve.wait_ge(taken, g + 1)
                    if f + 2 < KD:
                        w_part(f + 2)
                    if f % 2 == 1 and 0 < f // 2 < len(mods):
                        finish(f // 2)
    end_block(nc)


def layer_even(nc, e, hT):
    e.g_save = nc.dram_tensor("gates_save", [TS, 3 * H], F32, kind="Internal").ap()
    e.o_save = nc.dram_tensor("o_save", [TS, H * HD], F32, kind="Internal").ap()
    early = ExitStack()
    e.w_attn = early.enter_context(nc.sbuf_tensor("w_attn", [P, 2, KD, 512], F32, side="right"))
    with nc.sbuf_tensor("x_T", [P, KD, T], F32) as xT:
        block_load(nc, e, xT, hT)
        block_norm(nc, e, xT, hT, 0, "norm0", hT)
    with nc.sbuf_tensor("o_T", [P, 4, T], F32) as oT:
        A = Env()
        A.hT, A.oT = hT, oT
        with ExitStack() as ctx:
            def sb(name, shape, dt=F32):
                return ctx.enter_context(nc.sbuf_tensor(name, shape, dt))
            A.kvrow, A.QT = sb("kv_rows", [P, NT, 768]), sb("q_T", [P, HG, T])
            A.KT, A.gates = sb("k_T", [P, 2, NKEY + TS]), sb("gates", [P, NT, 3 * H])
            A.peT, A.kccT = sb("pe_T", [P, 2 * CB]), sb("k_cmp_T", [P, NKEY // CB])
            A.o_smp = sb("o_samples", [TS, H * HD])
            A.vcd, A.vcs = sb("v_cmp_diag", [P, G, HG * HD]), sb("v_cmp_samples", [NCS, DB, P])
            with nc.sbuf_tensor("cmp_in_T", [P, 2, NKEY], F32) as cmpT:
                A.cmpT = cmpT
                block_attn_proj(nc, e, hT, A)
                early.close()
                with nc.sbuf_tensor("v_past", [P, DB * NPG, 256], F32) as vpast:
                    A.vpast = vpast
                    block_past(nc, e, A)
                    A.w_za, A.w_za_in = early.enter_context(nc.sbuf_tensor("w_z_a", [P, KD, 512], F32, side="right")), nc.alloc_semaphore("w_z_a_in")
                    block_attn_samples(nc, e, A)
            block_attn_prompt(nc, e, A)
            early.close()
        S = Env()
        with ExitStack() as ctx:
            def sb(name, shape, dt=F32):
                return ctx.enter_context(nc.sbuf_tensor(name, shape, dt))
            S.convT = sb("conv_T", [P, KC, T])
            S.xd, S.dta, S.ea = sb("dt", [P, NT, SH]), sb("dt_a", [P, NT, SH]), sb("exp_a_log", [P, SH])
            S.w_zb, S.w_zb_in = early.enter_context(nc.sbuf_tensor("w_z_b", [P, KD, SI], F32, side="right")), nc.alloc_semaphore("w_z_b_in")
            block_ssd_proj(nc, e, hT, S)
            with nc.sbuf_tensor("h_state", [P, SI], F32) as h:
                S.h = h
                block_ssd_scan(nc, e, hT, S)
            block_ssd_samples(nc, e, hT, S)
            early.close()
            mix = [oT[:, k:k + 2, :] for k in (0, 2)] + [S.convT[:, k:k + 2, :] for k in (0, 2, 4, 6)]
            block_out(nc, e, "out_even", e.w_out_even[0], mix, 3, 0, hT, [(0, 2), (1, 0), (1, 1), (1, 2)])


def load_w_r(sp, e, Q, c):
    s = O_R + 512 * c
    sp.dma_start(Q.wr[c][:, :, :], e.w_in_odd[0, :, s:s + 512].rearrange("(k p) n -> p k n", p=P)).then_inc(Q.wr_in[c], 16)


def block_gla_proj(nc, e, h2, Q):
    NQ = 8 * 3
    with ExitStack() as ctx:
        def sb(name, shape, dt=F32):
            return ctx.enter_context(nc.sbuf_tensor(name, shape, dt))
        w, wg, wg2, scan = Q.w_qkv, Q.w_glr, Q.w_gate2, Q.scan
        glrT = sb("glr_T", [16, T])
        A, E = sb("gate_sums", [P, LH, T]), sb("gate_tmp", [P, 2, T])
        w_in, g_in = Q.w_in, Q.g_in
        sem = lambda s: new_sem(nc, "gla_" + s)
        glr_done, glr_ready, x_done, abs_taken, x_taken, qk_done, qk_taken, v_done, v_act, v_dve = (sem(s) for s in
            ("glr", "glr_ready", "x", "abs_taken", "x_taken", "qk", "qk_taken", "v", "v_taken_act", "v_taken_dve"))
        ln_ready, cum_ready, diff_ready, exp_ready, mult_done, khat_done = (sem(s) for s in ("ln", "cum", "diff", "exp", "mult", "khat"))
        with nc.Block() as block:
            @block.sync
            def _(sp):
                load_w_r(sp, e, Q, 0)
                for c in range(2, 8):
                    if c - 2 < 4:
                        sp.wait_ge(qk_done, 6 * (c - 1))
                    else:
                        sp.wait_ge(v_done, NT * (c - 5))
                    sp.dma_start(w[:, c % 2, :, :], e.w_in_odd[0, :, 256 * c:256 * (c + 1)].rearrange("(k p) n -> p k n", p=P)).then_inc(w_in[c % 2], 16)

            @block.tensor
            def _(pe):
                pe.wait_ge(g_in, 48)
                for c, (s, n) in enumerate(CHUNKS):
                    for k in range(KD):
                        last = mm(nc, e.ps[0:16, c, 0:n], wg[:, k, :], h2[:, k, s:s + n], k == 0, k == KD - 1)
                    last.then_inc(glr_done, 1)

                def gates(h):
                    if h:
                        pe.wait_ge(x_taken, h)
                    for c, (s, n) in enumerate(CHUNKS):
                        last = mm(nc, e.ps[:, 5 + c, 0:n], wg2[:, h * P:(h + 1) * P], glrT[:, s:s + n], True, True)
                    last.then_inc(x_done, 1)

                pe.wait_ge(glr_ready, 3)
                gates(0)
                for f in range(8):
                    if f % 2 == 0:
                        pe.wait_ge(w_in[f // 2 % 2], 16 * (f // 4 + 1))
                    for c, (s, n) in enumerate(CHUNKS):
                        g = 3 * f + c
                        if g >= 5:
                            pe.wait_ge(qk_taken, g - 4)
                        for k in range(KD):
                            last = mm(nc, e.ps[:, g % 5, 0:n], w[:, f // 2 % 2, k, (f % 2) * P:(f % 2 + 1) * P], h2[:, k, s:s + n], k == 0, k == KD - 1)
                        last.then_inc(qk_done, 1)
                    if f < LH - 1:
                        gates(f + 1)
                pe.wait_ge(qk_taken, NQ)
                for c in range(4):
                    pe.wait_ge(w_in[c % 2], 16 * (c // 2 + 3))
                    for m in range(NT):
                        g, r = c * NT + m, rows(m)
                        if g >= 4:
                            pe.wait_ge((v_act, v_dve)[g % 2], g // 2 - 1)
                        for k in range(KD):
                            last = mm(nc, e.ps[0:r, g % 4, 0:256], h2[:, k, m * P:m * P + r], w[:, c % 2, k, :], k == 0, k == KD - 1)
                        last.then_inc(v_done, 1)

            def v_copy(eng, copy, c, parity, sem_):
                for g in range(c * NT, (c + 1) * NT):
                    if g % 2 == parity:
                        m = g % NT
                        eng.wait_ge(v_done, g + 1)
                        copy(Q.V[0:rows(m), m, 256 * c:256 * (c + 1)], e.ps[0:rows(m), g % 4, 0:256]).then_inc(sem_, 1)

            @block.scalar
            def _(act):
                for c, (s, n) in enumerate(CHUNKS):
                    act.wait_ge(glr_done, c + 1)
                    nc.scalar.copy(glrT[:, s:s + n], e.ps[0:16, c, 0:n]).then_inc(glr_ready, 1)
                for f in range(8):
                    if f < LH:
                        b = e.vec[:, VEC["gla_b"][0] + f:VEC["gla_b"][0] + f + 1]
                        x = E[:, f % 2, :]
                        act.wait_ge(x_done, f + 1)
                        if f >= 2:
                            act.wait_ge(cum_ready, f - 1)
                        for c, (s, n) in enumerate(CHUNKS):
                            last = nc.scalar.activation(E[:, f % 2, s:s + n], e.ps[:, 5 + c, 0:n], ACT.Abs, bias=b)
                        last.then_inc(abs_taken, 1)
                        act.wait_ge(abs_taken, f + 1)
                        nc.scalar.activation(x, x, ACT.Exp, scale=-1.0).then_inc(ln_ready, 1)
                        act.wait_ge(ln_ready, 2 * f + 1)
                        nc.scalar.activation(x, x, ACT.Ln, bias=1.0).then_inc(ln_ready, 1)
                    for c, (s, n) in enumerate(CHUNKS):
                        g = 3 * f + c
                        act.wait_ge(qk_done, g + 1)
                        if f < LH:
                            nc.scalar.mul(Q.QK[:, 0, f, s:s + n], e.ps[:, g % 5, 0:n], LK ** -0.5).then_inc(qk_taken, 1)
                        else:
                            nc.scalar.copy(Q.QK[:, 1, f - LH, s:s + n], e.ps[:, g % 5, 0:n]).then_inc(qk_taken, 1)
                act.wait_ge(diff_ready, LH)
                for h in range(LH):
                    if h:
                        act.wait_ge(mult_done, 2 * h - 1)
                    nc.scalar.activation(E[:, 0, :], A[:, h, :], ACT.Exp, scale=1.0 / 16).then_inc(exp_ready, 1)
                    nc.scalar.activation(Q.eb[:, h, 0:TP // LC], A[:, h, LC - 1:TP:LC], ACT.Exp, scale=1.0 / 16)
                    nc.scalar.activation(Q.eb[:, h, TP // LC:], A[:, h, TP + DS - 1:T:DS], ACT.Exp, scale=1.0 / 16)
                    nc.scalar.activation(Q.KH[:, h, :], Q.KH[:, h, :], ACT.Exp, scale=1.0 / 16).then_inc(exp_ready, 1)
                    if h:
                        act.wait_ge(mult_done, 2 * h)
                    nc.scalar.activation(E[:, 1, :], A[:, h, :], ACT.Exp, scale=-1.0 / 16).then_inc(exp_ready, 1)
                    v_copy(act, nc.scalar.copy, h, 0, v_act)

            @block.gpsimd
            def _(pool):
                pool.wait_ge(qk_taken, NQ)
                for h in range(LH):
                    pool.wait_ge(exp_ready, 3 * h + 2)
                    nc.gpsimd.tensor_tensor(Q.KH[:, h, :], Q.KH[:, h, :], Q.QK[:, 1, h, :], ALU.mult).then_inc(khat_done, 1)

            @block.vector
            def _(dve):
                link = make_link(dve, e.dve_step, e.dve_n)
                dve.wait_ge(g_in, 48)
                for h in range(LH):
                    b = e.vec[:, VEC["gla_b"][0] + h:VEC["gla_b"][0] + h + 1]
                    dve.wait_ge(abs_taken, h + 1)
                    for c, (s, n) in enumerate(CHUNKS):
                        last = nc.vector.tensor_scalar(A[:, h, s:s + n], e.ps[:, 5 + c, 0:n], b, 0.0, ALU.add, ALU.min)
                    last.then_inc(x_taken, 1)
                    dve.wait_ge(x_taken, h + 1)
                    dve.wait_ge(ln_ready, 2 * h + 2)
                    link(nc.vector.tensor_tensor(E[:, h % 2, :], A[:, h, :], E[:, h % 2, :], ALU.subtract))
                    nc.vector.tensor_tensor_scan(A[:, h, :], scan[:, :], E[:, h % 2, :], 0.0, ALU.mult, ALU.add).then_inc(cum_ready, 1)
                    dve.wait_ge(cum_ready, h + 1)
                    for s, t, n, c in ((0, TP, TP // LC, LC), (TP, T, DB, DS)):
                        a = A[:, h, s:t].rearrange("p (n c) -> p n c", c=c)
                        last = nc.vector.tensor_tensor(Q.KH[:, h, s:t].rearrange("p (n c) -> p n c", c=c), a[:, :, c - 1:c].broadcast_to([P, n, c]), a, ALU.subtract)
                    last.then_inc(diff_ready, 1)
                dve.wait_ge(qk_taken, NQ)
                for h in range(LH):
                    for j in range(2):
                        dve.wait_ge(exp_ready, 3 * h + 1 + 2 * j)
                        if j:
                            dve.wait_ge(khat_done, h + 1)
                        nc.vector.tensor_tensor(Q.QK[:, j, h, :], Q.QK[:, j, h, :], E[:, j, :], ALU.mult).then_inc(mult_done, 1)
                    v_copy(dve, nc.vector.tensor_copy, h, 1, v_dve)
    end_block(nc)


def block_gla_scan(nc, e, h2, Q):
    with ExitStack() as ctx:
        def sb(name, shape, dt=F32):
            return ctx.enter_context(nc.sbuf_tensor(name, shape, dt))
        att = sb("att", [P, 2, LH, P])
        kr = sb("k_hat_rows", [P, 2, P // LC, LH, P])
        S = sb("gla_state", [P, 2, LH, LV])
        rs, og, junk, ss = sb("silu_r", [P, 2, LH * LV]), sb("o_gated", [P, 2, LH * LV]), sb("o_square", [P, LV]), sb("o_norm", [P, 2, LH])
        sem = lambda s: new_sem(nc, "glas_" + s)
        zeroed, att_done, att_ready, kr_ready, r_done, r_taken, intra_done, upd_done, s_ready, inter_done, sq_done, var_ready, std_ready, o_taken, o_gated, yT_done, yT_taken = \
            (sem(s) for s in ("zeroed", "att", "att_ready", "kr_ready", "r", "r_taken", "intra", "upd", "state_ready", "inter", "squared", "var", "std", "o_taken", "o_gated", "yT", "yT_taken"))
        NC = P // LC
        out = e.stored["gla_state"]
        mask = e.F["tri32"].bitcast(I32)[:, None, :].broadcast_to([P, LH, P])
        with nc.Block() as block:
            @block.sync
            def _(sp):
                load_w_r(sp, e, Q, 1)
                sp.wait_ge(s_ready, NTP * NC)
                sp.dma_start(e.outs[10][0, 0].rearrange("h k v -> k h v"), S[:, 0, :, :]).then_inc(out, 16)
                sp.wait_ge(out, 16)

            @block.tensor
            def _(pe):
                def yT(i):
                    pe.wait_ge(o_gated, i + 1)
                    if i + 1 < NTP:
                        pe.wait_ge(r_taken, i + 2)
                    for j in range(8):
                        last = nc.tensor.transpose(e.ps[:, 6 + j // 4, (j % 4) * P:(j % 4 + 1) * P], og[:, i % 2, j * P:(j + 1) * P], e.ident)
                    last.then_inc(yT_done, 1)

                pe.wait_ge(zeroed, 2)
                for i in range(NTP):
                    tok = slice(i * P, (i + 1) * P)
                    if i:
                        pe.wait_ge(att_ready, i)
                        pe.wait_ge(kr_ready, i)
                    for h in range(LH):
                        mm(nc, e.ps[:, 0, h * P:(h + 1) * P], Q.QK[:, 1, h, tok], Q.QK[:, 0, h, tok], True, True)
                    for h in range(LH):
                        last = nc.tensor.transpose(e.ps[:, 1, h * P:(h + 1) * P], Q.KH[:, h, tok], e.ident)
                    last.then_inc(att_done, 1)
                    if i == 1:
                        pe.wait_ge(r_taken, 1)
                    if i >= 2:
                        pe.wait_ge(yT_taken, i - 1)
                    for c in range(2):
                        if i == 0:
                            pe.wait_ge(Q.wr_in[c], 16)
                        for k in range(KD):
                            last = mm(nc, e.ps[:, 6 + c, :], h2[:, k, tok], Q.wr[c][:, k, :], k == 0, k == KD - 1)
                    last.then_inc(r_done, 1)
                    pe.wait_ge(att_ready, i + 1)
                    pe.wait_ge(kr_ready, i + 1)
                    if i:
                        pe.wait_ge(o_taken, i)
                    for h in range(LH):
                        mm(nc, e.ps[:, 4 + h // 2, (h % 2) * LV:(h % 2 + 1) * LV], att[:, i % 2, h, :], Q.V[:, i, h * LV:(h + 1) * LV], h % 2 == 0, False)
                    for j in range(NC):
                        n = i * NC + j
                        row = slice(j * LC, (j + 1) * LC)
                        pe.wait_ge(s_ready, n)
                        for h in range(LH):
                            last = mm(nc, e.ps[:, 2 + h // 2, (h % 2) * LV:(h % 2 + 1) * LV], kr[:, i % 2, j, h, :], Q.V[:, i, h * LV:(h + 1) * LV], True, True)
                        last.then_inc(upd_done, 1)
                        for h in range(LH):
                            last = mm(nc, e.ps[row, 4 + h // 2, (h % 2) * LV:(h % 2 + 1) * LV], Q.QK[:, 0, h, i * P + j * LC:i * P + (j + 1) * LC],
                                      S[:, n % 2, h, :], False, j == NC - 1)
                        last.then_inc(inter_done, 1)
                        if j == 1 and i:
                            yT(i - 1)
                pe.wait_ge(yT_taken, NTP - 1)
                yT(NTP - 1)

            @block.scalar
            def _(act):
                act.wait_ge(zeroed, 4)
                for i in range(NTP):
                    act.wait_ge(att_done, i + 1)
                    if i >= 2:
                        act.wait_ge(upd_done, NC * (i - 1))
                    for j in range(NC):
                        row = slice(j * LC, (j + 1) * LC)
                        last = nc.scalar.copy(kr[row, i % 2, j, :, :], e.ps[row, 1, :].rearrange("p (h d) -> p h d", h=LH))
                    last.then_inc(kr_ready, 1)
                    act.wait_ge(r_done, i + 1)
                    if i >= 2:
                        act.wait_ge(o_gated, i - 1)
                    nc.scalar.activation(rs[:, i % 2, :].rearrange("p (b n) -> p b n", b=2), e.ps[:, 6:8, :], ACT.Silu).then_inc(r_taken, 1)
                    act.wait_ge(inter_done, NC * (i + 1))
                    for h in range(LH):
                        if h:
                            act.wait_ge(sq_done, LH * i + h)
                        nc.scalar.activation(junk[:, :], e.ps[:, 4 + h // 2, (h % 2) * LV:(h % 2 + 1) * LV], ACT.Square, accum_out=ss[:, i % 2, h:h + 1]).then_inc(sq_done, 1)
                    act.wait_ge(var_ready, i + 1)
                    nc.scalar.activation(ss[:, i % 2, :], ss[:, i % 2, :], ACT.Sqrt).then_inc(std_ready, 1)

            @block.gpsimd
            def _(pool):
                nc.gpsimd.memset(att[:, :, :, :], 0.0).then_inc(zeroed, 1)
                nc.gpsimd.memset(S[:, 0, :, :], 0.0).then_inc(zeroed, 1)
                for i in range(2):
                    nc.gpsimd.memset(kr[:, i], 0.0).then_inc(zeroed, 1)
                for i in range(NTP):
                    pool.wait_ge(o_taken, i + 1)
                    nc.gpsimd.tensor_tensor(og[:, i % 2, :], og[:, i % 2, :], rs[:, i % 2, :], ALU.mult).then_inc(o_gated, 1)

            @block.vector
            def _(dve):
                link = make_link(dve, e.dve_step, e.dve_n)

                def put_yT(i):
                    dve.wait_ge(yT_done, i + 1)
                    s = VEC["gla_norm"][0]
                    w = e.vec[:, s:s + 2][:, None, :, None].broadcast_to([P, 2, 2, P])
                    for c in range(2):
                        last = nc.vector.tensor_tensor(h2[:, 4 * c:4 * c + 4, i * P:(i + 1) * P].rearrange("p (h x) t -> p h x t", x=2),
                                                       e.ps[:, 6 + c, :].rearrange("p (h x t) -> p h x t", h=2, x=2), w, ALU.mult)
                    last.then_inc(yT_taken, 1)

                dve.wait_ge(zeroed, 2)
                for i in range(NTP):
                    dve.wait_ge(att_done, i + 1)
                    nc.vector.copy_predicated(att[:, i % 2, :, :], mask, e.ps[:, 0, :].rearrange("p (h t) -> p h t", h=LH)).then_inc(att_ready, 1)
                    for j in range(NC):
                        n = i * NC + j
                        dve.wait_ge(upd_done, n + 1)
                        if n:
                            dve.wait_ge(inter_done, n)
                        for h in range(LH):
                            last = nc.vector.scalar_tensor_tensor(S[:, (n + 1) % 2, h, :], S[:, n % 2, h, :], Q.eb[:, h, n:n + 1],
                                                                  e.ps[:, 2 + h // 2, (h % 2) * LV:(h % 2 + 1) * LV], ALU.mult, ALU.add)
                        last.then_inc(s_ready, 1)
                        dve.wait_ge(s_ready, n + 1)
                        if j == 1 and i:
                            put_yT(i - 1)
                    dve.wait_ge(sq_done, LH * (i + 1))
                    link(nc.vector.tensor_scalar(ss[:, i % 2, :], ss[:, i % 2, :], 1.0 / LV, EPS, ALU.mult, ALU.add))
                    nc.vector.reciprocal(ss[:, i % 2, :], ss[:, i % 2, :]).then_inc(var_ready, 1)
                    dve.wait_ge(std_ready, i + 1)
                    if i >= 2:
                        dve.wait_ge(yT_taken, i - 1)
                    nc.vector.tensor_tensor(og[:, i % 2, :].rearrange("p (h v) -> p h v", h=LH), e.ps[:, 4:6, :].rearrange("p b (h v) -> p (b h) v", h=2),
                                            ss[:, i % 2, :][:, :, None].broadcast_to([P, LH, LV]), ALU.mult).then_inc(o_taken, 1)
                put_yT(NTP - 1)
    end_block(nc)


def block_gla_samples(nc, e, h2, Q):
    R = TS
    tok = slice(TP, T)
    with ExitStack() as ctx:
        def sb(name, shape, dt=F32):
            return ctx.enter_context(nc.sbuf_tensor(name, shape, dt))
        att, kr = sb("att_s", [R, LH, R]), sb("k_hat_rows_s", [R, LH, P])
        qm, km = sb("q_masked", [P, LH, DB, R]), sb("k_hat_masked", [R, DB, LH, P])
        S, N = sb("gla_state_in", [P, 2, LH, LV]), sb("gla_state_new", [P, 2, LH, LV])
        rs, og, junk, ss = sb("silu_r_s", [R, LH * LV]), sb("o_gated_s", [R, LH * LV]), sb("o_square_s", [R, LV]), sb("o_norm_s", [R, LH])
        sem = lambda s: new_sem(nc, "glab_" + s)
        zeroed, att_done, att_ready, kr_ready, km_ready, qm_ready, r_done, r_taken = (sem(s) for s in ("zeroed", "att", "att_ready", "kr_ready", "km", "qm", "r", "r_taken"))
        s_in, st_out, upd_done, new_ready, inter_done, sq_done, var_ready, std_ready, o_taken, o_gated, yT_done = \
            ([sem("in0"), sem("in1")], [e.stored["gla_states0"], e.stored["gla_states1"]], *(sem(s) for s in ("upd", "new", "inter", "squared", "var", "std", "o_taken", "o_gated", "yT")))
        mask = e.F["trib"][0:R, :].bitcast(I32)[:, None, :].broadcast_to([R, LH, R])
        with nc.Block() as block:
            @block.sync
            def _(sp):
                for b in range(DB):
                    if b >= 2:
                        sp.wait_ge(inter_done, b - 1)
                        sp.wait_ge(new_ready, b - 1)
                    sp.dma_start(S[:, b % 2, :, :], e.state_gla[0, b].rearrange("h k v -> k h v")).then_inc(s_in[b % 2], 16)

            @block.tensor
            def _(pe):
                for h in range(LH):
                    mm(nc, e.ps[0:R, 0, h * R:(h + 1) * R], Q.QK[:, 1, h, tok], Q.QK[:, 0, h, tok], True, True)
                for h in range(LH):
                    last = nc.tensor.transpose(e.ps[0:R, 1, h * P:(h + 1) * P], Q.KH[:, h, tok], e.ident)
                last.then_inc(att_done, 1)
                for c in range(2):
                    for k in range(KD):
                        last = mm(nc, e.ps[0:R, 6 + c, :], h2[:, k, tok], Q.wr[c][:, k, :], k == 0, k == KD - 1)
                last.then_inc(r_done, 1)
                pe.wait_ge(att_ready, 1)
                for h in range(LH):
                    mm(nc, e.ps[0:R, 4 + h // 2, (h % 2) * LV:(h % 2 + 1) * LV], att[:, h, :], Q.V[0:R, NTP, h * LV:(h + 1) * LV], h % 2 == 0, False)
                pe.wait_ge(km_ready, 1)
                pe.wait_ge(qm_ready, 1)
                for b in range(DB):
                    pe.wait_ge(s_in[b % 2], 16 * (b // 2 + 1))
                    if b:
                        pe.wait_ge(new_ready, b)
                    for h in range(LH):
                        last = mm(nc, e.ps[:, 2 + h // 2, (h % 2) * LV:(h % 2 + 1) * LV], km[:, b, h, :], Q.V[0:R, NTP, h * LV:(h + 1) * LV], True, True)
                    last.then_inc(upd_done, 1)
                    for h in range(LH):
                        last = mm(nc, e.ps[0:R, 4 + h // 2, (h % 2) * LV:(h % 2 + 1) * LV], qm[:, h, b, :], S[:, b % 2, h, :], False, b == DB - 1)
                    last.then_inc(inter_done, 1)
                pe.wait_ge(o_gated, 1)
                for j in range(8):
                    last = nc.tensor.transpose(e.ps[:, 0, j * R:(j + 1) * R], og[:, j * P:(j + 1) * P], e.ident[0:R, 0:R])
                last.then_inc(yT_done, 1)

            @block.scalar
            def _(act):
                act.wait_ge(att_done, 1)
                nc.scalar.copy(kr[:, :, :], e.ps[0:R, 1, :].rearrange("p (h d) -> p h d", h=LH)).then_inc(kr_ready, 1)
                act.wait_ge(r_done, 1)
                nc.scalar.activation(rs[:, :].rearrange("p (b n) -> p b n", b=2), e.ps[0:R, 6:8, :], ACT.Silu).then_inc(r_taken, 1)
                for b in range(DB):
                    act.wait_ge(new_ready, b + 1)
                    act.dma_start(e.outs[11][0, b].rearrange("h k v -> k h v"), N[:, b % 2, :, :]).then_inc(st_out[b % 2], 16)
                act.wait_ge(inter_done, DB)
                for h in range(LH):
                    if h:
                        act.wait_ge(sq_done, h)
                    nc.scalar.activation(junk[:, :], e.ps[0:R, 4 + h // 2, (h % 2) * LV:(h % 2 + 1) * LV], ACT.Square, accum_out=ss[:, h:h + 1]).then_inc(sq_done, 1)
                act.wait_ge(var_ready, 1)
                nc.scalar.activation(ss[:, :], ss[:, :], ACT.Sqrt).then_inc(std_ready, 1)
                for b in range(2):
                    act.wait_ge(st_out[b], 16 * DB // 2)

            @block.gpsimd
            def _(pool):
                nc.gpsimd.memset(att[:, :, :], 0.0).then_inc(zeroed, 1)
                for h in range(LH):
                    last = nc.gpsimd.tensor_tensor(qm[:, h, :, :], Q.QK[:, 0, h, tok][:, None, :].broadcast_to([P, DB, R]),
                                                   e.F["bmask"].rearrange("p (b t) -> p b t", b=DB), ALU.mult)
                last.then_inc(qm_ready, 1)
                pool.wait_ge(kr_ready, 1)
                for h in range(LH):
                    last = nc.gpsimd.tensor_tensor(km[:, :, h, :], kr[:, h, :][:, None, :].broadcast_to([R, DB, P]),
                                                   e.F["bcol"][0:R, :][:, :, None].broadcast_to([R, DB, P]), ALU.mult)
                last.then_inc(km_ready, 1)
                pool.wait_ge(o_taken, 1)
                pool.wait_ge(r_taken, 1)
                nc.gpsimd.tensor_tensor(og[:, :], og[:, :], rs[:, :], ALU.mult).then_inc(o_gated, 1)

            @block.vector
            def _(dve):
                link = make_link(dve, e.dve_step, e.dve_n)
                dve.wait_ge(att_done, 1)
                dve.wait_ge(zeroed, 1)
                nc.vector.copy_predicated(att[:, :, :], mask, e.ps[0:R, 0, 0:LH * R].rearrange("p (h t) -> p h t", h=LH)).then_inc(att_ready, 1)
                for b in range(DB):
                    dve.wait_ge(upd_done, b + 1)
                    if b >= 2:
                        dve.wait_ge(st_out[b % 2], 16 * (b // 2))
                    for h in range(LH):
                        last = nc.vector.scalar_tensor_tensor(N[:, b % 2, h, :], S[:, b % 2, h, :], Q.eb[:, h, TP // LC + b:TP // LC + b + 1],
                                                              e.ps[:, 2 + h // 2, (h % 2) * LV:(h % 2 + 1) * LV], ALU.mult, ALU.add)
                    last.then_inc(new_ready, 1)
                dve.wait_ge(sq_done, LH)
                link(nc.vector.tensor_scalar(ss[:, :], ss[:, :], 1.0 / LV, EPS, ALU.mult, ALU.add))
                nc.vector.reciprocal(ss[:, :], ss[:, :]).then_inc(var_ready, 1)
                dve.wait_ge(std_ready, 1)
                nc.vector.tensor_tensor(og[:, :].rearrange("p (h v) -> p h v", h=LH), e.ps[0:R, 4:6, :].rearrange("p b (h v) -> p (b h) v", h=2),
                                        ss[:, :][:, :, None].broadcast_to([R, LH, LV]), ALU.mult).then_inc(o_taken, 1)
                dve.wait_ge(yT_done, 1)
                s = VEC["gla_norm"][0]
                link(nc.vector.tensor_tensor(h2[:, :, tok].rearrange("p (h x) t -> p h x t", x=2), e.ps[:, 0, 0:8 * R].rearrange("p (h x t) -> p h x t", h=4, x=2),
                                             e.vec[:, s:s + 2][:, None, :, None].broadcast_to([P, 4, 2, R]), ALU.mult))
    end_block(nc)


def block_store(nc, e, yT):
    NG = NT * 2
    with ExitStack() as ctx:
        y = ctx.enter_context(nc.sbuf_tensor("y_out", [P, 4, D], F32))
        turned, ya, yd, out = new_sem(nc, "y_turned"), new_sem(nc, "y_copied_act"), new_sem(nc, "y_copied_dve"), [e.stored[f"y{i}"] for i in range(4)]
        with nc.Block() as block:
            @block.tensor
            def _(pe):
                for g in range(NG):
                    m, half = g // 2, g % 2
                    r = rows(m)
                    if g >= 8:
                        pe.wait_ge((yd, ya)[g % 2], g // 2 - 3)
                    for j in range(4):
                        last = nc.tensor.transpose(e.ps[0:r, g % 8, j * P:(j + 1) * P], yT[:, 4 * half + j, m * P:m * P + r], e.ident)
                    last.then_inc(turned, 1)

            def copies(eng, copy, half, sem_):
                for m in range(NT):
                    g, r = 2 * m + half, rows(m)
                    eng.wait_ge(turned, g + 1)
                    if m >= 4:
                        eng.wait_ge(out[m % 4], 16 * (m // 4))
                    copy(y[0:r, m % 4, 512 * half:512 * (half + 1)], e.ps[0:r, g % 8, :]).then_inc(sem_, 1)

            @block.scalar
            def _(act):
                copies(act, nc.scalar.copy, 1, ya)

            @block.vector
            def _(dve):
                copies(dve, nc.vector.tensor_copy, 0, yd)

            @block.sync
            def _(sp):
                for m in range(NT):
                    sp.wait_ge(ya, m + 1)
                    sp.wait_ge(yd, m + 1)
                    dst = e.outs[0][0, m * P:(m + 1) * P, :] if m < NTP else e.outs[1].rearrange("b t d -> (b t) d")
                    sp.dma_start(dst, y[0:rows(m), m % 4, :]).then_inc(out[m % 4], 16)
                for i in range(4):
                    sp.wait_ge(out[i], 16 * len(range(i, NT, 4)))
    end_block(nc)


def layer_odd(nc, e, hT):
    with nc.sbuf_tensor("h2_T", [P, KD, T], F32) as h2:
        Q = Env()
        early = ExitStack()

        def right(name, shape):
            return early.enter_context(nc.sbuf_tensor(name, shape, F32, side="right"))

        Q.wr, Q.wr_in = [right("w_r0", [P, KD, 512])], [nc.alloc_semaphore(f"w_r_in{c}") for c in range(2)]
        with ExitStack() as first:
            def right1(name, shape):
                return first.enter_context(nc.sbuf_tensor(name, shape, F32, side="right"))

            Q.w_qkv, Q.w_glr = right1("w_qkv", [P, 2, KD, 256]), right1("w_glr", [P, KD, 16])
            Q.w_gate2, Q.scan = right1("w_gate2", [16, LH * LK]), right1("scan_mask", [P, T])
            Q.w_in, Q.g_in = [nc.alloc_semaphore(f"w_qkv_in{i}") for i in range(2)], nc.alloc_semaphore("w_glr_in")

            def first_weights(sp):
                sp.dma_start(Q.w_glr[:, :, :], e.w_in_odd[0, :, O_GLR:O_R].rearrange("(k p) n -> p k n", p=P)).then_inc(Q.g_in, 16)
                sp.dma_start(Q.w_gate2[:, :], e.gla_w_gate2[0]).then_inc(Q.g_in, 16)
                sp.dma_start(Q.scan[:, :], e.k_scan).then_inc(Q.g_in, 16)
                for c in range(2):
                    sp.dma_start(Q.w_qkv[:, c, :, :], e.w_in_odd[0, :, 256 * c:256 * (c + 1)].rearrange("(k p) n -> p k n", p=P)).then_inc(Q.w_in[c], 16)

            block_norm(nc, e, hT, h2, 1, "norm1", h2, save=True, loads=first_weights)
            ctx = ExitStack()
            Q.QK = hT[:, :, :].rearrange("p (a h) t -> p a h t", a=2)
            Q.KH = ctx.enter_context(nc.sbuf_tensor("k_hat_T", [P, LH, T], F32))
            Q.V = ctx.enter_context(nc.sbuf_tensor("v_rows", [P, NT, LH * LV], F32))
            Q.eb = ctx.enter_context(nc.sbuf_tensor("chunk_decay", [P, LH, TP // LC + DB], F32))
            block_gla_proj(nc, e, h2, Q)
        with ctx, early:
            Q.wr.append(ctx.enter_context(nc.sbuf_tensor("w_r1", [P, KD, 512], F32)))
            block_gla_scan(nc, e, h2, Q)
            block_gla_samples(nc, e, h2, Q)
        block_out(nc, e, "out_odd", e.w_out_odd[0], [h2[:, k:k + 2, :] for k in range(0, KD, 2)], 4, 1, hT)
        block_norm(nc, e, hT, h2, None, "norm2", h2)
        block_store(nc, e, h2)


def build(nc, a, outs):
    e = Env()
    e.x_prompt, e.x_sample, e.c_prompt, e.c_sample = a["x_prompt"], a["x_sample"], a["c_prompt"], a["c_sample"]
    e.cache_nsa, e.cache_nsa_win, e.state_ssd_conv, e.state_ssd = a["cache_nsa"], a["cache_nsa_win"], a["state_ssd_conv"], a["state_ssd"]
    e.state_gla, e.page_table, e.norm_w, e.w_mod = a["state_gla"], a["page_table"], a["norm_w"], a["w_mod"]
    e.b_mod, e.w_in_even, e.w_out_even, e.nsa_cmp_pe = a["b_mod"], a["w_in_even"], a["w_out_even"], a["nsa_cmp_pe"]
    e.nsa_cmp_w1, e.nsa_cmp_w2, e.ssd_conv_w, e.ssd_conv_b = a["nsa_cmp_w1"], a["nsa_cmp_w2"], a["ssd_conv_w"], a["ssd_conv_b"]
    e.ssd_dt_bias, e.ssd_a_log, e.ssd_d, e.ssd_norm_w = a["ssd_dt_bias"], a["ssd_a_log"], a["ssd_d"], a["ssd_norm_w"]
    e.w_in_odd, e.gla_w_gate2, e.gla_b_gate, e.gla_norm_w = a["w_in_odd"], a["gla_w_gate2"], a["gla_b_gate"], a["gla_norm_w"]
    e.w_out_odd, e.final_norm_w, e.k_f32, e.k_masks = a["w_out_odd"], a["final_norm_w"], a["k_f32"], a["k_masks"]
    e.k_rope, e.k_scan = a["k_rope"], a["k_scan"]
    e.outs = outs
    e.x_save = nc.dram_tensor("x_T_save", [P, KD, T], F32, kind="Internal").ap()
    with ExitStack() as ctx:
        def sb(name, shape, dt=F32):
            return ctx.enter_context(nc.sbuf_tensor(name, shape, dt))
        e.ps = ctx.enter_context(nc.psum_tensor("banks", [P, 8, 512], F32))
        e.kf, e.kb = sb("const_f32", [P, F_WIDTH]), sb("const_bf16", [P, B_WIDTH], BF16)
        e.ident = e.kf[:, 0:P]
        e.identb = e.kb[:, 0:P]
        e.F = {k: e.kf[:, s:t] for k, (s, t) in F_COLS.items()}
        e.B = {k: e.kb[:, s:t] for k, (s, t) in B_COLS.items()}
        e.vec = sb("vectors", [P, NVEC + NCW])
        e.mod = sb("modulation", [P, 2, 3 * KD, 9])
        e.cT = e.mod[:, 1, 2 * KD:3 * KD, :]
        e.ssd_row = sb("ssd_rows", [P, 3, SH])
        e.dve_step, e.dve_n = nc.alloc_semaphore("dve_step"), [0]
        e.act_step, e.act_n = nc.alloc_semaphore("act_step"), [0]
        e.pool_step, e.pool_n = nc.alloc_semaphore("pool_step"), [0]
        e.stored = {n: nc.alloc_semaphore("stored_" + n) for n in ("kv_rows", "conv", "ssd_state", "ssd_states0", "ssd_states1",
                                                                   "gla_state", "gla_states0", "gla_states1", "y0", "y1", "y2", "y3")}
        hT = sb("h_T", [P, KD, T])
        e.w_attn_in = [nc.alloc_semaphore(f"w_attn_in{i}") for i in range(2)]
        layer_even(nc, e, hT)
        layer_odd(nc, e, hT)


_INS = ["x_prompt", "x_sample", "c_prompt", "c_sample", "cache_nsa", "cache_nsa_win", "state_ssd_conv", "state_ssd",
        "state_gla", "page_table", "norm_w", "w_mod", "b_mod", "w_in_even", "w_out_even", "nsa_cmp_pe", "nsa_cmp_w1",
        "nsa_cmp_w2", "ssd_conv_w", "ssd_conv_b", "ssd_dt_bias", "ssd_a_log", "ssd_d", "ssd_norm_w", "w_in_odd",
        "gla_w_gate2", "gla_b_gate", "gla_norm_w", "w_out_odd", "final_norm_w"]
_OUTS = [(1, TP, D), (DB, DS, D), (1, 1, TP, 4, G, HD), (1, DB, DS, 4, G, HD), (1, 1, WIN, 2, G, HD),
         (1, DB, PAST, 2, G, HD), (1, 1, 3, CCH), (1, DB, 3, CCH), (1, 1, SH, SP_, SN), (1, DB, SH, SP_, SN),
         (1, 1, LH, LK, LV), (1, DB, LH, LK, LV)]


def kernel(**inputs):
    import concourse.bacc as _bacc
    from concourse.bass_utils import run_bass_kernel_spmd as _run

    nc = _bacc.Bacc("TRN2", target_bir_lowering=False, num_devices=1)
    arrays, args, outs = {}, {}, []
    given = {name: np.ascontiguousarray(inputs[name]) for name in _INS}
    for name, v in {**given, **shape_constants()}.items():
        arrays[f"in_{name}_dram"] = v
        args[name] = nc.dram_tensor(f"in_{name}_dram", v.shape, mybir.dt.from_np(v.dtype), kind="ExternalInput").ap()
    for i, shape in enumerate(_OUTS):
        outs.append(nc.dram_tensor(f"out_{i}_dram", shape, F32, kind="ExternalOutput").ap())
    build(nc, args, outs)
    r = _run(nc, [arrays], core_ids=[0])
    return tuple(r.results[0][f"out_{i}_dram"] for i in range(len(_OUTS)))
```
